# Optimizing a Trainium2 kernel written in Bass

```python
import jax, jax.numpy as jnp
from jax import lax
import numpy as np

D_MODEL = 1024
BATCH = 1
SEQ = 512
DEPTH = 1

GRID_W = 64
POOL_WINDOWS = (2, 4, 8, 16)
POOL_WIDTH = D_MODEL // 2
POOL_GROUP = POOL_WIDTH // len(POOL_WINDOWS)
ATTN_HEADS = 8
HEAD_DIM = (D_MODEL // 2) // ATTN_HEADS
ATTN_WIDTH = ATTN_HEADS * HEAD_DIM
MIX_WIDTH = POOL_WIDTH + ATTN_WIDTH
WIN_ROWS_MAX = 8
WIN_COLS = 16
N_EXPERTS = 16
EC_CAPACITY = 2
D_EXPERT = 2 * D_MODEL
PLE_DIM = 256
RMS_EPS = 1e-6


def rms_norm(x, g):
    x32 = x.astype(jnp.float32)
    y = x32 * lax.rsqrt(jnp.mean(x32 * x32, axis=-1, keepdims=True) + RMS_EPS)
    return (y * g.astype(jnp.float32)).astype(x.dtype)

def multiscale_pool(u, w_pool, pool_scale):
    B, S, _ = u.shape
    u32 = u.astype(jnp.float32)
    cs = jnp.concatenate([jnp.zeros((B, 1, POOL_WIDTH), jnp.float32), jnp.cumsum(u32, axis=1)], axis=1)
    t = jnp.arange(S)
    outs = []
    for gi, w in enumerate(POOL_WINDOWS):
        lo = jnp.clip(t - w // 2, 0, S - 1)
        hi = jnp.clip(t + (w - w // 2) - 1, 0, S - 1)
        sl = slice(gi * POOL_GROUP, (gi + 1) * POOL_GROUP)
        csg = cs[:, :, sl]
        cnt = (hi - lo + 1).astype(jnp.float32)[None, :, None]
        outs.append((csg[:, hi + 1] - csg[:, lo]) / cnt - u32[:, :, sl])
    d = jnp.stack(outs, axis=2).astype(u.dtype)
    y = jnp.einsum('bsgc,gcd->bsgd', d, w_pool).reshape(B, S, POOL_WIDTH)
    return y * pool_scale

def neighbourhood_attention(q, k, v, q_norm, k_norm, rpb):
    B, S, H, HD = q.shape
    rows = S // GRID_W
    kh = min(WIN_ROWS_MAX, rows)
    q = rms_norm(q, q_norm) * (HD ** -0.5)
    k = rms_norm(k, k_norm)
    to_grid = lambda a: a.reshape(B, rows, GRID_W, H, HD).transpose(0, 3, 1, 2, 4)
    qg, kg, vg = to_grid(q), to_grid(k), to_grid(v)
    c = jnp.arange(GRID_W)
    col_start = jnp.clip(c - WIN_COLS // 2, 0, GRID_W - WIN_COLS)
    col_idx = col_start[:, None] + jnp.arange(WIN_COLS)[None, :]
    dc = col_idx - c[:, None] + (WIN_COLS - 1)

    def row_block(r):
        row_start = jnp.clip(r - kh // 2, 0, rows - kh)
        q_r = lax.dynamic_index_in_dim(qg, r, axis=2, keepdims=False)
        k_band = lax.dynamic_slice_in_dim(kg, row_start, kh, axis=2)
        v_band = lax.dynamic_slice_in_dim(vg, row_start, kh, axis=2)
        k_nb = k_band[:, :, :, col_idx]
        v_nb = v_band[:, :, :, col_idx]
        s = jnp.einsum('bhcd,bhicjd->bhcij', q_r, k_nb).astype(jnp.float32)
        dr = row_start + jnp.arange(kh) - r + (WIN_ROWS_MAX - 1)
        bias = rpb[:, dr[None, :, None], dc[:, None, :]]
        s = s + bias[None].astype(jnp.float32)
        pr = jax.nn.softmax(s.reshape(B, H, GRID_W, kh * WIN_COLS), axis=-1)
        pr = pr.reshape(B, H, GRID_W, kh, WIN_COLS).astype(v.dtype)
        return jnp.einsum('bhcij,bhicjd->bhcd', pr, v_nb)

    o = lax.map(row_block, jnp.arange(rows))
    return o.transpose(1, 0, 3, 2, 4).reshape(B, S, H * HD)

def expert_choice_ffn(h, w_router, w_gate, w_up, w_down):
    B, S, D = h.shape
    cap = EC_CAPACITY * S // N_EXPERTS
    aff = jax.nn.softmax(jnp.einsum('bsd,de->bse', h, w_router).astype(jnp.float32), axis=-1)
    gates, idx = lax.top_k(aff.transpose(0, 2, 1), cap)
    bidx = jnp.arange(B)[:, None, None]
    xe = h[bidx, idx]
    a = jnp.einsum('becd,edf->becf', xe, w_gate)
    b = jnp.einsum('becd,edf->becf', xe, w_up)
    ye = jnp.einsum('becf,efd->becd', jax.nn.silu(a) * b, w_down)
    return jnp.zeros_like(h).at[bidx, idx].add(ye * gates[..., None].astype(h.dtype))

def first_inputs(seed: int = 0) -> dict:
    key = jax.random.key(seed)
    ks = jax.random.split(key, 20)
    f32 = jnp.float32
    nrm = lambda k, shape, s: jax.random.normal(k, shape, f32) * s
    gain = lambda k, shape: 1.0 + 0.02 * jax.random.normal(k, shape, f32)
    L = DEPTH
    return {
        "x": nrm(ks[0], (BATCH, SEQ, D_MODEL), 1.0),
        "p": nrm(ks[1], (L, BATCH, SEQ, PLE_DIM), 1.0),
        "norm_mix": gain(ks[2], (L, D_MODEL)),
        "w_in": nrm(ks[3], (L, D_MODEL, POOL_WIDTH + 3 * ATTN_WIDTH), D_MODEL ** -0.5),
        "w_pool": nrm(ks[4], (L, len(POOL_WINDOWS), POOL_GROUP, POOL_GROUP), POOL_GROUP ** -0.5),
        "pool_scale": gain(ks[5], (L, POOL_WIDTH)),
        "q_norm": gain(ks[6], (L, HEAD_DIM)),
        "k_norm": gain(ks[7], (L, HEAD_DIM)),
        "rpb": nrm(ks[8], (L, ATTN_HEADS, 2 * WIN_ROWS_MAX - 1, 2 * WIN_COLS - 1), 0.1),
        "w_out": nrm(ks[9], (L, MIX_WIDTH, D_MODEL), MIX_WIDTH ** -0.5),
        "norm_ffn": gain(ks[10], (L, D_MODEL)),
        "w_router": nrm(ks[11], (L, D_MODEL, N_EXPERTS), D_MODEL ** -0.5),
        "w_gate": nrm(ks[12], (L, N_EXPERTS, D_MODEL, D_EXPERT), D_MODEL ** -0.5),
        "w_up": nrm(ks[13], (L, N_EXPERTS, D_MODEL, D_EXPERT), D_MODEL ** -0.5),
        "w_down": nrm(ks[14], (L, N_EXPERTS, D_EXPERT, D_MODEL), D_EXPERT ** -0.5),
        "norm_ple": gain(ks[15], (L, D_MODEL)),
        "w_ple_gate": nrm(ks[16], (L, D_MODEL, D_MODEL), D_MODEL ** -0.5),
        "w_ple_proj": nrm(ks[17], (L, PLE_DIM, D_MODEL), PLE_DIM ** -0.5),
        "norm_ple_post": gain(ks[18], (L, D_MODEL)),
    }

def first_block(x, p, norm_mix, w_in, w_pool, pool_scale, q_norm, k_norm, rpb, w_out,
              norm_ffn, w_router, w_gate, w_up, w_down, norm_ple, w_ple_gate,
              w_ple_proj, norm_ple_post):
    B, S, _ = x.shape
    for i in range(DEPTH):
        h = rms_norm(x, norm_mix[i])
        z = h @ w_in[i]
        u = z[..., :POOL_WIDTH]
        qkv = z[..., POOL_WIDTH:].reshape(B, S, 3, ATTN_HEADS, HEAD_DIM)
        y_pool = multiscale_pool(u, w_pool[i], pool_scale[i])
        y_attn = neighbourhood_attention(qkv[:, :, 0], qkv[:, :, 1], qkv[:, :, 2],
                                         q_norm[i], k_norm[i], rpb[i])
        x = x + jnp.concatenate([y_pool, y_attn], axis=-1) @ w_out[i]
        x = x + expert_choice_ffn(rms_norm(x, norm_ffn[i]), w_router[i], w_gate[i], w_up[i], w_down[i])
        g = jax.nn.sigmoid(rms_norm(x, norm_ple[i]) @ w_ple_gate[i])
        e = rms_norm(p[i] @ w_ple_proj[i], norm_ple_post[i])
        x = x + g * e
    return x


DEPTH_2 = 2

N_A_LAYERS = DEPTH_2 // 2
N_B_LAYERS = DEPTH_2 - N_A_LAYERS
EPS = 1e-6

CHUNK = 128
A_WIDTH = 2 * D_MODEL
A_GROUP_WIDTH = 256
A_GROUPS = A_WIDTH // A_GROUP_WIDTH

HEAD_DIM_2 = 128
DILATED_GROUPS = ((128, 1), (512, 4), (2048, 16))
N_GROUPS = len(DILATED_GROUPS)
Q_HEADS_PER_GROUP = D_MODEL // HEAD_DIM_2
KV_HEADS_PER_GROUP = 2
Q_PER_KV = Q_HEADS_PER_GROUP // KV_HEADS_PER_GROUP
N_Q_HEADS = N_GROUPS * Q_HEADS_PER_GROUP
N_KV_HEADS = N_GROUPS * KV_HEADS_PER_GROUP
B_WIDTH = Q_HEADS_PER_GROUP * HEAD_DIM_2
BAND = 128


def rms_norm_2(x, g):
    xf = x.astype(jnp.float32)
    y = xf * lax.rsqrt(jnp.mean(xf * xf, axis=-1, keepdims=True) + EPS)
    return (y * g.astype(jnp.float32)).astype(x.dtype)

def ada_mod(c, w, b, n):
    h = jax.nn.silu(c) @ w + b
    return jnp.split(h[:, None, :], n, axis=-1)

def alibi_slopes():
    h = jnp.arange(1, N_Q_HEADS + 1, dtype=jnp.float32)
    return jnp.exp2(-8.0 * h / N_Q_HEADS)

def to_dilated(t, d):
    b, s = t.shape[:2]
    rest = t.shape[2:]
    span = d * BAND
    sp = -(-s // span) * span
    t = jnp.pad(t, [(0, 0), (0, sp - s)] + [(0, 0)] * len(rest))
    t = t.reshape((b, sp // d, d) + rest)
    t = jnp.swapaxes(t, 1, 2)
    return t.reshape((b, d, sp // span, BAND) + rest)

def from_dilated(t, s):
    b, d, nb = t.shape[:3]
    rest = t.shape[4:]
    t = t.reshape((b, d, nb * BAND) + rest)
    t = jnp.swapaxes(t, 1, 2)
    return t.reshape((b, nb * BAND * d) + rest)[:, :s]

def band_keys(t):
    prev = jnp.pad(t[:, :, :-1], [(0, 0), (0, 0), (1, 0)] + [(0, 0)] * 3)
    return jnp.concatenate([prev, t], axis=3)

def gmlp_layer(x, c, ada_w, ada_b, norm_g, w_in, sgu_g, w_s, b_s, w_out):
    bsz, s, _ = x.shape
    shift, scale, gate = ada_mod(c, ada_w, ada_b, 3)
    h = rms_norm_2(x, norm_g) * (1 + scale) + shift
    u, v, z = jnp.split(h @ w_in, 3, axis=-1)
    u = jax.nn.gelu(u)
    v = rms_norm_2(jax.nn.gelu(v), sgu_g)
    v = v.reshape(bsz, s // CHUNK, CHUNK, A_GROUPS, A_GROUP_WIDTH)
    w_causal = jnp.tril(w_s)
    mixed = jnp.einsum('gts,bcsge->bctge', w_causal, v) + b_s.T[None, None, :, :, None]
    y = u * mixed.reshape(bsz, s, A_WIDTH) * jax.nn.silu(z)
    return x + gate * (y @ w_out)

def shared_kv(x, c, ada_w, ada_b, norm_g, w_kv, k_norm_g):
    bsz, s, _ = x.shape
    shift, scale = ada_mod(c, ada_w, ada_b, 2)
    h = rms_norm_2(x, norm_g) * (1 + scale) + shift
    k, v = jnp.split(h @ w_kv, 2, axis=-1)
    k = rms_norm_2(k.reshape(bsz, s, N_KV_HEADS, HEAD_DIM_2), k_norm_g)
    v = v.reshape(bsz, s, N_KV_HEADS, HEAD_DIM_2)
    groups = []
    for g, (window, d) in enumerate(DILATED_GROUPS):
        hs = slice(g * KV_HEADS_PER_GROUP, (g + 1) * KV_HEADS_PER_GROUP)
        groups.append((band_keys(to_dilated(k[:, :, hs], d)),
                       band_keys(to_dilated(v[:, :, hs], d))))
    return groups

def dilated_group_attn(q, kb, vb, slopes, window, d):
    s = q.shape[1]
    ql = to_dilated(q, d)
    bsz, _, nb = ql.shape[:3]
    ql = ql.reshape(bsz, d, nb, BAND, KV_HEADS_PER_GROUP, Q_PER_KV, HEAD_DIM_2)
    sc = jnp.einsum('brnikgh,brnjkh->brnkgij', ql, kb, preferred_element_type=jnp.float32)
    i = jnp.arange(BAND)[:, None]
    j = jnp.arange(2 * BAND)[None, :]
    dq = BAND + i - j
    key_idx = (jnp.arange(nb)[:, None, None] - 1) * BAND + j
    valid = (dq >= 0) & (dq <= window // d) & (key_idx >= 0)
    bias = -slopes.astype(jnp.float32).reshape(KV_HEADS_PER_GROUP, Q_PER_KV)[:, :, None, None] \
        * (d * dq).astype(jnp.float32)
    sc = jnp.where(valid[:, None, None], sc + bias, -jnp.inf)
    m = jnp.max(sc, axis=-1, keepdims=True)
    p = jnp.exp(sc - m)
    l = jnp.sum(p, axis=-1, keepdims=True)
    o = jnp.einsum('brnkgij,brnjkh->brnikgh', p / l, vb.astype(jnp.float32))
    lse = jnp.moveaxis((m + jnp.log(l))[..., 0], -1, 3)
    o = from_dilated(o.reshape(bsz, d, nb, BAND, Q_HEADS_PER_GROUP, HEAD_DIM_2), s)
    lse = from_dilated(lse.reshape(bsz, d, nb, BAND, Q_HEADS_PER_GROUP), s)
    return o, lse

def dilated_layer(x, c, kv_groups, ada_w, ada_b, norm_g, w_in, q_norm_g, w_out):
    bsz, s, _ = x.shape
    shift, scale, gate = ada_mod(c, ada_w, ada_b, 3)
    h = rms_norm_2(x, norm_g) * (1 + scale) + shift
    qz = h @ w_in
    q = qz[..., :N_Q_HEADS * HEAD_DIM_2].reshape(bsz, s, N_Q_HEADS, HEAD_DIM_2)
    z = qz[..., N_Q_HEADS * HEAD_DIM_2:]
    q = rms_norm_2(q, q_norm_g) * (HEAD_DIM_2 ** -0.5)
    slopes = alibi_slopes()
    outs, lses = [], []
    for g, (window, d) in enumerate(DILATED_GROUPS):
        hs = slice(g * Q_HEADS_PER_GROUP, (g + 1) * Q_HEADS_PER_GROUP)
        kb, vb = kv_groups[g]
        o, lse = dilated_group_attn(q[:, :, hs], kb, vb, slopes[hs], window, d)
        outs.append(o)
        lses.append(lse)
    alpha = jax.nn.softmax(jnp.stack(lses), axis=0)
    o = jnp.sum(alpha[..., None] * jnp.stack(outs), axis=0).astype(x.dtype)
    y = o.reshape(bsz, s, B_WIDTH) * jax.nn.silu(z)
    return x + gate * (y @ w_out)

def second_inputs(seed: int = 0) -> dict:
    key = jax.random.key(seed)
    ks = jax.random.split(key, 24)
    nrm = lambda k, shape, sc: jax.random.normal(k, shape, jnp.float32) * sc
    D = D_MODEL
    return {
        "x": nrm(ks[0], (BATCH, SEQ, D), 1.0),
        "c": nrm(ks[1], (BATCH, D), 1.0),
        "a_ada_w": nrm(ks[2], (N_A_LAYERS, D, 3 * D), 0.5 * D ** -0.5),
        "a_ada_b": nrm(ks[3], (N_A_LAYERS, 3 * D), 0.01),
        "a_norm_g": 1.0 + nrm(ks[4], (N_A_LAYERS, D), 0.05),
        "a_w_in": nrm(ks[5], (N_A_LAYERS, D, 3 * A_WIDTH), D ** -0.5),
        "a_sgu_g": 1.0 + nrm(ks[6], (N_A_LAYERS, A_WIDTH), 0.05),
        "a_w_spatial": nrm(ks[7], (N_A_LAYERS, A_GROUPS, CHUNK, CHUNK), 0.5 * CHUNK ** -0.5),
        "a_b_spatial": 1.0 + nrm(ks[8], (N_A_LAYERS, A_GROUPS, CHUNK), 0.01),
        "a_w_out": nrm(ks[9], (N_A_LAYERS, A_WIDTH, D), A_WIDTH ** -0.5),
        "kv_ada_w": nrm(ks[10], (D, 2 * D), 0.5 * D ** -0.5),
        "kv_ada_b": nrm(ks[11], (2 * D,), 0.01),
        "kv_norm_g": 1.0 + nrm(ks[12], (D,), 0.05),
        "w_kv": nrm(ks[13], (D, 2 * N_KV_HEADS * HEAD_DIM_2), D ** -0.5),
        "k_norm_g": 1.0 + nrm(ks[14], (HEAD_DIM_2,), 0.05),
        "b_ada_w": nrm(ks[15], (N_B_LAYERS, D, 3 * D), 0.5 * D ** -0.5),
        "b_ada_b": nrm(ks[16], (N_B_LAYERS, 3 * D), 0.01),
        "b_norm_g": 1.0 + nrm(ks[17], (N_B_LAYERS, D), 0.05),
        "b_w_in": nrm(ks[18], (N_B_LAYERS, D, N_Q_HEADS * HEAD_DIM_2 + B_WIDTH), D ** -0.5),
        "b_q_norm_g": 1.0 + nrm(ks[19], (N_B_LAYERS, HEAD_DIM_2), 0.05),
        "b_w_out": nrm(ks[20], (N_B_LAYERS, B_WIDTH, D), B_WIDTH ** -0.5),
    }

def second_block(x, c, a_ada_w, a_ada_b, a_norm_g, a_w_in, a_sgu_g, a_w_spatial, a_b_spatial,
              a_w_out, kv_ada_w, kv_ada_b, kv_norm_g, w_kv, k_norm_g, b_ada_w, b_ada_b,
              b_norm_g, b_w_in, b_q_norm_g, b_w_out):
    kv_groups = None
    for layer in range(DEPTH_2):
        if layer < N_A_LAYERS:
            x = gmlp_layer(x, c, a_ada_w[layer], a_ada_b[layer], a_norm_g[layer], a_w_in[layer],
                           a_sgu_g[layer], a_w_spatial[layer], a_b_spatial[layer], a_w_out[layer])
        else:
            if layer == N_A_LAYERS:
                kv_groups = shared_kv(x, c, kv_ada_w, kv_ada_b, kv_norm_g, w_kv, k_norm_g)
            lb = layer - N_A_LAYERS
            x = dilated_layer(x, c, kv_groups, b_ada_w[lb], b_ada_b[lb], b_norm_g[lb], b_w_in[lb],
                              b_q_norm_g[lb], b_w_out[lb])
    return x


def setup_inputs(seed=0):
    out = dict(first_inputs(seed))
    for name, value in second_inputs(seed + 1).items():
        if name != "x":
            out[name + "_2"] = value
    return out


def reference(
    x, p, norm_mix, w_in, w_pool, pool_scale, q_norm, k_norm, rpb, w_out, norm_ffn, w_router,
    w_gate, w_up, w_down, norm_ple, w_ple_gate, w_ple_proj, norm_ple_post, c_2, a_ada_w_2,
    a_ada_b_2, a_norm_g_2, a_w_in_2, a_sgu_g_2, a_w_spatial_2, a_b_spatial_2, a_w_out_2,
    kv_ada_w_2, kv_ada_b_2, kv_norm_g_2, w_kv_2, k_norm_g_2, b_ada_w_2, b_ada_b_2, b_norm_g_2,
    b_w_in_2, b_q_norm_g_2, b_w_out_2,
):
    x = first_block(
        x, p, norm_mix, w_in, w_pool, pool_scale, q_norm, k_norm, rpb, w_out, norm_ffn,
        w_router, w_gate, w_up, w_down, norm_ple, w_ple_gate, w_ple_proj, norm_ple_post,
    )
    return second_block(
        x, c_2, a_ada_w_2, a_ada_b_2, a_norm_g_2, a_w_in_2, a_sgu_g_2, a_w_spatial_2,
        a_b_spatial_2, a_w_out_2, kv_ada_w_2, kv_ada_b_2, kv_norm_g_2, w_kv_2, k_norm_g_2,
        b_ada_w_2, b_ada_b_2, b_norm_g_2, b_w_in_2, b_q_norm_g_2, b_w_out_2,
    )


_drawn_inputs = setup_inputs


def setup_inputs(seed=0):
    import zlib

    import numpy as np

    out = dict(_drawn_inputs(seed))
    spreads = {}
    factors = {'norm_mix': 4.053,
     'pool_scale': 4.054,
     'q_norm': 8.0,
     'k_norm': 8.0,
     'rpb': 5.334,
     'norm_ffn': 4.328,
     'norm_ple': 8.0,
     'norm_ple_post': 6.953,
     'a_ada_b_2': 8.0,
     'a_norm_g_2': 6.822,
     'a_sgu_g_2': 8.0,
     'a_b_spatial_2': 8.0,
     'kv_ada_b_2': 8.0,
     'kv_norm_g_2': 8.0,
     'k_norm_g_2': 8.0,
     'b_ada_b_2': 8.0,
     'b_norm_g_2': 8.0,
     'b_q_norm_g_2': 8.0}
    for name, (base, spread) in spreads.items():
        noise = np.random.default_rng([zlib.crc32(name.encode()), seed]).standard_normal(out[name].shape)
        drawn = base * np.exp(spread * noise) if base else spread * noise
        out[name] = __import__('jax').numpy.asarray(drawn.astype(out[name].dtype))
    for name, factor in factors.items():
        out[name] = (out[name] * factor).astype(out[name].dtype)
    return out
```

```python
from contextlib import ExitStack

import numpy as np

import concourse.bass as bass
from concourse import mybir

P = 128
D = 1024
KD = D // P
S = 512
NT = S // P
HD1, H1 = 64, 8
ROWS, COLS = 8, 64
WIN = 16
NE, CAP, F = 16, 64, 2048
H2, NG, KV2 = 8, 3, 2
EPS = 1e-6
NEG = -1e30
RING = 4
SLAB = 2048
SLABS_E = 24

F32, F32R, BF16 = mybir.dt.float32, mybir.dt.float32r, mybir.dt.bfloat16
ALU = mybir.AluOpType
ACT = mybir.ActivationFunctionType
AX = mybir.AxisListType

COL_ROWS = (("norm_mix", KD), ("norm_ple", KD), ("a_norm_g_2", KD), ("kv_norm_g_2", KD),
            ("b_norm_g_2", KD), ("pool_scale", 4), ("a_sgu_g_2", 16), ("a_ada_b_2", 16),
            ("kv_ada_b_2", 16), ("b_ada_b_2", 16), ("q_norm", 1), ("k_norm", 1),
            ("b_q_norm_g_2", 1), ("k_norm_g_2", 1), ("c_2", KD))
COL = {}
_n = 0
for _name, _rows in COL_ROWS:
    COL[_name] = _n
    _n += _rows
NCOL = _n


def grid_constants():
    i = np.arange(P)
    ident = np.eye(P, dtype=np.float32)
    blocks = (i[:, None] // HD1 == i[None, :] // HD1).astype(np.float32)
    jmod = np.broadcast_to((i % CAP + 1).astype(np.float32), (P, P))
    stack = (i[:, None] % CAP == np.arange(CAP)[None, :]).astype(np.float32)
    tril = (i[:, None] <= i[None, :]).astype(np.float32)
    far = 1e30
    dq0 = np.concatenate([P + i[:, None] - i[None, :], i[:, None] - i[None, :]], axis=1)
    d0 = np.where((dq0 >= 0) & (dq0 <= 128), dq0, far).astype(np.float32)
    dq = i[:, None] - i[None, :]
    d1 = np.where(dq >= 0, 4.0 * dq, far).astype(np.float32)
    d2 = np.where((dq % 4 == 0) & (dq >= 0), 4.0 * dq, far).astype(np.float32)
    early = np.concatenate([ident, blocks, jmod, stack], axis=1)
    late = np.concatenate([d0, d1, d2, tril], axis=1)

    def window(t, kts):
        c = 16 * t + 15 - i // ROWS
        start = np.clip(c - WIN // 2, 0, COLS - WIN)
        kc = (np.concatenate([16 * k + np.arange(16) for k in kts]))
        ok = (kc[None, :] >= start[:, None]) & (kc[None, :] < start[:, None] + WIN)
        return np.repeat(np.where(ok, 0.0, NEG), ROWS, axis=1)
    wins = np.concatenate([window(1, (0, 1, 2)), window(0, (0, 1)), window(3, (2, 3)), ident], axis=1)
    t = np.arange(S)
    cnt = []
    for w in (2, 4, 8, 16):
        lo = np.clip(t - w // 2, 0, S - 1)
        hi = np.clip(t + (w - w // 2) - 1, 0, S - 1)
        cnt.append(1.0 / (hi - lo + 1))
    return early, late, wins, np.stack(cnt).astype(np.float32)



def bass_kernel(nc, a, out, stop=99):

    early, late, wins, invcnt = grid_constants()
    c_early = nc.inline_tensor(early, name="c_early").ap()
    c_late = nc.inline_tensor(late, name="c_late").ap()
    c_wins = nc.inline_tensor(wins.astype(mybir.dt.np(BF16)), name="c_wins").ap()
    c_cnt = nc.inline_tensor(invcnt, name="c_cnt").ap()
    rpb_wide = nc.dram_tensor("rpb_wide", (ROWS, H1 * ROWS, 63), F32, kind="Internal").ap()

    with ExitStack() as ctx:
        base = (nc.sbuf_base + 31) // 32 * 32

        def at(name, kb, shape, dt=F32):
            return nc.alloc_sbuf_tensor_at(name, shape, dt, offset=base + int(kb * 1024))

        X = at("x_res", 0, [P, NT, D])
        RAW = [at(f"raw{i}", 16 + 8 * i, [P, SLAB]) for i in range(RING)]
        WHI = [at(f"w_hi{i}", 48 + 8 * i, [P, SLAB], F32R) for i in range(2)]
        WLO = [at(f"w_lo{i}", 64 + 8 * i, [P, SLAB], F32R) for i in range(2)]
        AH = at("act_hi", 80, [P, KD, S], F32R)
        AL = at("act_lo", 96, [P, KD, S], F32R)
        BH = at("mix_hi", 112, [P, KD, S], F32R)
        BL = at("mix_lo", 128, [P, KD, S], F32R)
        WHI_E = WHI + [at("w_hi2", 172, [P, SLAB], F32R)]
        WLO_E = WLO + [at("w_lo2", 180, [P, SLAB], F32R)]
        XN = at("x_norm", 112, [P, NT, D])
        FULL = [at(f"full{i}", 144 + 2 * i, [P, S]) for i in range(2)]
        SQ = [at(f"square{i}", 148 + 2 * i, [P, S]) for i in range(2)]
        ROWS_IN = at("param_rows", 140, [P, P])
        UP = at("u_padded", 152, [P, 4, S + 16])
        Q1 = at("q1", 160.5, [P, 4, S])
        K1 = at("k1", 168.5, [P, 4, S])
        V1 = at("v1", 176.5, [P, NT, 512])
        BIAS = at("bias_master", 184.5, [P, H1 * ROWS, 48])
        RPB = at("rpb_padded", 132, [H1, 15, 63])
        ACC1 = at("ada_acc1", 136, [P, D])
        W2 = at("win2", 80, [P, S + 16])
        W4 = at("win4", 82.5, [P, S + 16])
        W8 = at("win8", 85, [P, S + 16])
        W16 = at("win16", 87.5, [P, S + 16])
        DT = at("pool_d", 90, [P, 4, S])
        WP = at("w_pool_sb", 98, [P, 4, P])
        CNT = at("cnt_row", 100, [P, 512])
        S1 = [at(f"s1_{i}", 102 + 1.5 * i, [P, 384]) for i in range(2)]
        P1 = [at(f"p1_{i}", 105 + 1.5 * i, [P, 384]) for i in range(2)]
        PT1 = [at(f"pt1_{i}", 108 + 1.5 * i, [P, 384]) for i in range(2)]
        O1 = at("o1", 112 + 8, [P, NT, 512])
        TH = at("tok_hi", 80, [P, NT, D], F32R)
        TL = at("tok_lo", 96, [P, NT, D], F32R)
        GS = at("gate_rows", 112, [P, D])
        US = at("up_rows", 116, [P, D])
        XE = at("chosen", 120, [P, KD, P], F32R)
        HM = at("hidden", 124, [P, 2 * KD, P], F32R)
        Y = at("expert_out", 132, [P, D])
        SELG = at("sel_gated", 136, [P, NT, P])
        SELT = at("sel_gated_t", 138, [P, S])
        SEL = at("sel", 140, [P, NT, CAP], F32R)
        GROW = at("gain_row", 152, [P, D])
        E_ = at("ple_e", 156, [P, NT, D])
        PH = at("p_hi", 172, [P, 2, S], F32R)
        PL = at("p_lo", 176, [P, 2, S], F32R)
        PTOK = at("p_tok", 180, [P, NT, 256])
        WORK = [at(f"topk_work{i}", 184 + 2 * i, [NE, S]) for i in range(2)]
        MASK = at("topk_mask", 188, [NE, S])
        RANK = at("topk_rank", 190, [NE, S])
        WR = at("w_router_sb", 192, [P, KD, NE])
        AFF = at("affinity", 192.5, [P, NT, NE + 1])
        POS = at("position", 193, [P, NT, NE + 1])
        VV = at("v_rows", 152, [P, NT, 2 * D])
        WST = at("w_spatial_t", 184, [P, 8, P])
        WS_IN = at("w_spatial_in", 128, [P, 8, P])
        ACC2 = at("ada_acc2", 188, [P, D])
        GATE_B = at("gate_b", 192, [P, D])
        BS = [at(f"b_spatial{i}", 196 + 0.5 * i, [P, P]) for i in range(2)]
        K2 = at("k2", 152, [P, NG, KV2, S])
        V2 = at("v2", 164, [P, NG, NT, KV2 * P])
        Q2 = at("q2", 176, [P, H2, S])
        O2 = [at("o2_0", 112, [P, H2, NT, P]), at("o2_1", 128, [P, H2, NT, P]), at("o2_2", 176, [P, H2, NT, P])]
        NM2 = at("negmax2", 196, [P, NG, NT * H2])
        L2 = at("rowsum2", 196.375, [P, NG, NT * H2])
        NT2 = [at(f"negmax2_t{g}", 152 + 2 * g, [H2, S]) for g in range(NG)]
        LT2 = [at(f"rowsum2_t{g}", 158 + 2 * g, [H2, S]) for g in range(NG)]
        DG = [at(f"diag{i}", 164 + 6 * i, [P, NG * NT, P]) for i in range(2)]
        S2 = [at(f"s2_{i}", 144 + i, [P, 256]) for i in range(2)]
        P2 = [at(f"p2_{i}", 146 + i, [P, 256]) for i in range(2)]
        PT2 = [at(f"pt2_{i}", 148 + i, [P, 256]) for i in range(2)]
        MIN2 = at("min2", 150, [H2, S])
        GATE_A = at("gate_a", 197, [P, D])
        CE = at("const_early", 201, [P, 3 * P + CAP])
        CL = at("const_late", 202.75, [P, 5 * P])
        CW = at("const_wins", 202.75, [P, 896 + P], BF16)
        PCOL = at("param_cols", 205.25, [P, P])
        ONES = at("ones", 205.75, [P, P])
        ST = at("stats", 206.25, [P, 160])
        ident, blocks64, jmod = CE[:, 0:P], CE[:, P:2 * P], CE[:, 2 * P:3 * P]
        stack64 = CE[:, 3 * P:3 * P + CAP]
        ident_bf = CW[:, 896:896 + P]

        def st(i, n=1):
            return ST[:, i:i + n]
        SS, MS, STD, RSTD = st(0, 4), st(4, 4), st(8, 4), st(12, 4)
        QG1, KG1, QG2, KG2 = st(16), st(17), st(18), st(19)
        CSIL, CEXP = st(20, 8), st(28, 8)
        NM = [st(36), st(37)]
        RS = [st(38), st(39)]
        RR = [st(40), st(41)]
        EPSC = st(42)
        ESS, ERSTD = st(44, 4), st(48, 4)
        ADC = {k: st(56 + 8 * i, 8) for i, k in enumerate(("a_add", "a_mul", "kv_add", "kv_mul", "b_add", "b_mul"))}
        ADT = st(104, 8)
        SSV = st(112, 16)

        def pcol(name, k=0, n=1):
            return PCOL[:, COL[name] + k:COL[name] + k + n]

        NORM_MUL = {0: lambda k: pcol("norm_mix", k), 2: lambda k: pcol("norm_ple", k),
                    3: lambda k: ADC["a_mul"][:, k:k + 1], 4: lambda k: ADC["kv_mul"][:, k:k + 1],
                    5: lambda k: ADC["b_mul"][:, k:k + 1]}
        NORM_ADD = {3: lambda k: ADC["a_add"][:, k:k + 1], 4: lambda k: ADC["kv_add"][:, k:k + 1],
                    5: lambda k: ADC["b_add"][:, k:k + 1]}

        def bc(ap, off, n):
            return bass.AP(ap.tensor, ap.offset + off, [[0, P], [1, n]])

        def spread(ap, n):
            return bass.AP(ap.tensor, ap.offset, [list(ap.ap[0]), list(ap.ap[1]), [0, n]])

        def repeat(ap, n):
            return bass.AP(ap.tensor, ap.offset, [list(ap.ap[0]), [0, n], list(ap.ap[1])])

        def ada_done(i):
            return 11 * (i // 4) + 3 * (i % 4) + 2 if i >= 0 else 0

        stream, n_of, before = [], {"W": [], "A": []}, {}

        def slab(kind, src):
            stream.append((src, kind, len(n_of[kind])))
            n_of[kind].append(len(stream) - 1)
            return len(n_of[kind]) - 1

        def fm_src(w, c0):
            return w.rearrange("(k p) n -> p k n", p=P)[:, :, c0:c0 + 256]

        def tm_src(w, k0, c0):
            return w.rearrange("(k p) n -> p k n", p=P)[:, k0:k0 + 4, c0:c0 + 512]

        def wide_src(w, k0, c0):
            return w.rearrange("(k p) n -> p k n", p=P)[:, k0:k0 + 2, c0:c0 + D]

        ada_src = [wide_src(w, k, b * D)
                   for w, nb in ((a["a_ada_w_2"][0], 3), (a["kv_ada_w_2"], 2), (a["b_ada_w_2"][0], 3))
                   for b in range(nb) for k in range(0, KD, 2)]

        def ada_slabs(n):
            for _ in range(n):
                if len(n_of["A"]) < len(ada_src):
                    slab("A", ada_src[len(n_of["A"])])

        def tm_slabs(w, k0=0, cols=2, c0=0):
            return [[slab("W", tm_src(w, k0 + 4 * s, c0 + 512 * h)) for s in range(2)] for h in range(cols)]

        w_in, w_a, w_b = a["w_in"][0], a["a_w_in_2"][0], a["b_w_in_2"][0]
        W_IN = []
        for i in range(6):
            W_IN.append(slab("W", fm_src(w_in, 256 * i)))
            ada_slabs(2)
        W_V = tm_slabs(w_in, 0, 1, 1536)
        W_OUT = tm_slabs(a["w_out"][0])
        W_PROJ = slab("W", wide_src(a["w_ple_proj"][0], 0, 0))
        N_E, WE0 = len(stream), len(n_of["W"])
        for _ in range(NE * SLABS_E):
            slab("W", None)
        W_PGATE = tm_slabs(a["w_ple_gate"][0])
        W_AV = []
        for h in range(4):
            W_AV += tm_slabs(w_a, 0, 1, 2048 + 512 * h)
            ada_slabs(4)
        W_AU, W_AZ, W_AO = [], [], []
        for hh in range(2):
            for g in range(4 * hh, 4 * hh + 4):
                W_AU.append(slab("W", fm_src(w_a, 256 * g)))
                W_AZ.append(slab("W", fm_src(w_a, 4096 + 256 * g)))
                if g >= 0:
                    ada_slabs(1)
            W_AO.append(tm_slabs(a["a_w_out_2"][0], 8 * hh))
        assert len(n_of["A"]) == len(ada_src)
        W_K = [slab("W", fm_src(a["w_kv_2"], 256 * g)) for g in range(NG)]
        W_VK = [slab("W", fm_src(a["w_kv_2"], 768 + 256 * g)) for g in range(NG)]
        W_Q = [[slab("W", fm_src(w_b, 1024 * g + 256 * i)) for i in range(4)] for g in range(NG)]
        W_Z = [slab("W", fm_src(w_b, 3072 + 256 * i)) for i in range(4)]
        W_BO = tm_slabs(a["b_w_out_2"][0])

        order, fills, count = [], {}, {"act": 0, "dve": 0}
        ring0 = [0]

        def note(key, eng):
            count[eng] += 1
            fills[key] = (len(order), eng, count[eng], ring0[0])
            order.append(key)

        def note_norm(k):
            for kc in range(KD):
                note(("norm", k, kc), "act")
                if k == 1 and kc == 1:
                    note(("logits",), "dve")

        def note_attn(tag, n):
            for j in range(n + 2):
                if j < n:
                    note((tag + "s", j), "dve")
                if 1 <= j <= n:
                    note((tag + "t", j - 1), "act")
                if j >= 2:
                    note((tag + "o", j - 2), "dve")

        note(("cols",), "dve")
        note_norm(0)
        for j in range(12):
            note(("in", j), "act" if j < 4 else "dve")
            if j >= 5:
                note(("inss", j - 1), "act")
            if j == 5:
                note(("ada", 0), "dve")
            if j == 9:
                note(("ada", 1), "dve")
        note(("inss", 11), "act")
        for t in range(NT):
            note(("v", t), "act")
        note(("ada", 2, 0), "dve")
        note(("ada", 2, 1), "dve")
        ITEMS1 = [(t, h) for t in range(NT) for h in range(H1)]
        note_attn("a1", len(ITEMS1))
        for g in range(4):
            note(("pool", g), "act")
        for c in range(4):
            note(("ot1", c), "act")
        for h in range(2):
            for t in range(NT):
                note(("wout", h, t), "dve")
        note_norm(1)
        note(("aff_t",), "dve")
        for c in range(2):
            note(("pt", c), "act")
        for h in range(2):
            for t in range(NT):
                note(("proj", h, t), "act")
        note(("pos_t",), "dve")
        N_BEFORE_E, ring0[0] = len(order), len(order)
        COUNT_BEFORE_E = dict(count)
        note_norm(2)
        for h in range(2):
            for t in range(NT):
                note(("pgate", h, t), "act")
        note_norm(3)
        for i in range(2):
            note(("ws", i), "dve")
        for h in range(4):
            for t in range(NT):
                note(("av", h, t), "act")
            if h in (1, 2, 3):
                note(("ada", h + 2), "dve")
        for g in range(8):
            for c in range(2):
                note(("am", g, c), "dve")
            for c in range(2):
                note(("au", g, c), "dve")
            for c in range(2):
                note(("az", g, c), "dve")
            if g == 0:
                note(("ada", 6), "dve")
            if g == 3:
                note(("ada", 7, 0), "dve")
                note(("ada", 7, 1), "dve")
            if g % 4 == 3:
                for h in range(2):
                    for t in range(NT):
                        note(("ao", g // 4, h, t), "dve")
        note_norm(4)
        for j in range(6):
            note(("k2", j), "dve")
            if j >= 1:
                note(("k2ss", j - 1), "act")
        note(("k2ss", 5), "act")
        for g in range(NG):
            for t in range(NT):
                note(("v2", g, t), "act")
        note_norm(5)
        for g in range(NG):
            for j in range(H2):
                note(("q2", g, j), "dve")
                if j >= 1:
                    note(("q2ss", g, j - 1), "act")
            note(("q2ss", g, H2 - 1), "act")
            note_attn(f"b{g}", NT * H2)
        for g in range(NG):
            note(("nm_t", g), "dve")
            note(("l_t", g), "dve")
        for g in range(NG):
            note(("wg", g), "dve")
        for h in range(H2):
            note(("z", h), "act")
            note(("comb", h), "dve")
        for h in range(2):
            for t in range(NT):
                note(("bo", h, t), "dve")

        def bank(key):
            i, _, _, r0 = fills[key]
            return PS[(i - r0) % 8]

        def fill_no(key):
            return fills[key][0] + 1

        PS = [ctx.enter_context(nc.psum_tensor(f"bank{i}", [P, 512], F32)) for i in range(8)]

        def sem(name):
            return ctx.enter_context(nc.semaphore(name))

        loaded = [sem(f"slab_loaded{i}") for i in range(RING)]
        hi_ready, lo_ready = sem("w_hi_ready"), sem("w_lo_ready")
        half_used, e_used = sem("first_slab_used"), sem("expert_slab_used")
        filled = sem("bank_filled")
        freed = {"act": sem("bank_read_by_act"), "dve": sem("bank_read_by_dve")}
        ada_step = sem("ada_step")
        s_const, s_rows, s_x = sem("consts_loaded"), sem("rows_loaded"), sem("x_loaded")
        s_wins, s_ga, s_wp, s_cnt = sem("windows_loaded"), sem("gate_a_bias"), sem("w_pool_loaded"), sem("counts_loaded")
        s_rpb, s_pad, s_bias = sem("rpb_loaded"), sem("rpb_zeroed"), sem("bias_loaded")
        s_init, s_cols, s_csil, s_cexp = sem("dve_init"), sem("cols_ready"), sem("c_silu"), sem("c_exp")
        n_sq, n_ms, n_sqrt, n_rstd, n_xn = (sem(x) for x in ("norm_sq", "norm_ms", "norm_sqrt", "norm_rstd", "norm_x"))
        f_hi, f_lo = sem("split_hi"), sem("split_lo")
        h_sq, h_rec = sem("head_sq"), sem("head_rec")
        p_step = sem("pool_step")
        a_nm, a_exp, a_rr = sem("neg_max"), sem("exp_done"), sem("row_rec")
        s_grow, s_late, s_wr, s_p = sem("gain_row"), sem("late_loaded"), sem("router_loaded"), sem("p_loaded")
        t_hi, t_lo = sem("tok_hi"), sem("tok_lo")
        r_used, k_step, k_exp = sem("router_step"), sem("topk_step"), sem("router_exp")
        x_upd = sem("x_updated")
        s_store = sem("stored")
        m_g, m_u, m_t, m_d, m_x, m_s, m_c = (sem(x) for x in ("e_gate_mm", "e_up_mm", "e_turned", "e_down_mm", "e_gathered", "e_sel_turned", "e_combined"))
        v_gu, v_silu, v_xe, v_st, v_y = (sem(x) for x in ("e_rows_out", "e_silu", "e_chosen", "e_sel_t", "e_y"))
        d_selg, d_sel, d_cur, d_prod, d_hi, d_lo, d_add = (sem(x) for x in ("e_selg", "e_sel", "e_cur", "e_prod", "e_hid_hi", "e_hid_lo", "e_added"))
        g_small, s_ws, s_bs, s_gb = sem("gmlp_step"), sem("w_spatial_loaded"), [sem("b_spatial0"), sem("b_spatial1")], sem("gate_b_bias")
        c_step, c_exp = sem("merge_step"), sem("merge_exp")

        used_by, halves = {}, [0]

        def tm_used(ws, key):
            halves[0] += 1
            used_by[ws[0]] = (half_used, halves[0])
            used_by[ws[1]] = (filled, fill_no(key))

        for i, w in enumerate(W_IN):
            used_by[w] = (filled, fill_no(("in", 2 * i + 1)))
        tm_used(W_V[0], ("v", 3))
        for h in range(2):
            tm_used(W_OUT[h], ("wout", h, 3))
        used_by[W_PROJ] = (filled, fill_no(("proj", 1, 3)))
        for i in range(NE * SLABS_E):
            used_by[WE0 + i] = (e_used, i + 4)
        for h in range(2):
            tm_used(W_PGATE[h], ("pgate", h, 3))
        for h in range(4):
            tm_used(W_AV[h], ("av", h, 3))
        for g in range(8):
            used_by[W_AU[g]] = (filled, fill_no(("au", g, 1)))
            used_by[W_AZ[g]] = (filled, fill_no(("az", g, 1)))
            if g % 4 == 3:
                for h in range(2):
                    tm_used(W_AO[g // 4][h], ("ao", g // 4, h, 3))
        for g in range(NG):
            used_by[W_K[g]] = (filled, fill_no(("k2", 2 * g + 1)))
            used_by[W_VK[g]] = (filled, fill_no(("v2", g, 3)))
        for g in range(NG):
            for i in range(4):
                used_by[W_Q[g][i]] = (filled, fill_no(("q2", g, 2 * i + 1)))
        for i in range(4):
            used_by[W_Z[i]] = (filled, fill_no(("z", 2 * i + 1)))
        for h in range(2):
            tm_used(W_BO[h], ("bo", h, 3))

        def slot(n):
            return n % RING

        def raw3(n, k):
            return RAW[slot(n)][:, :].rearrange("p (k n) -> p k n", k=k)

        def tile_of(ap, g, t):
            if g == 0:
                return ap[:, t * P:(t + 1) * P]
            return ap.rearrange("p (i r) -> p r i", r=NT)[:, t, :]

        def to_order(ap, g):
            return ap if g == 0 else ap.rearrange("p (i r) -> p r i", r=NT)

        def in_order(ap, g):
            return ap if g == 0 else ap.rearrange("p (r i) -> p r i", r=NT)

        KEYS1 = {0: (0, 1), 1: (0, 1, 2), 2: (1, 2, 3), 3: (2, 3)}
        WINC = {0: 384, 1: 0, 2: 0, 3: 640}
        BJ = {0: 16, 1: 0, 2: 0, 3: 0}

        def item1(j):
            tr, h = ITEMS1[j]
            t = NT - 1 - tr
            kts = KEYS1[t]
            return tr, t, h, kts, len(kts) * P

        def item2(g, j):
            t, h = j // H2, j % H2
            kts = (t - 1, t) if g == 0 and t > 0 else (t,)
            return t, h, kts, len(kts) * P

        slopes = [2.0 ** (-8.0 * (i + 1) / (NG * H2)) for i in range(NG * H2)]


        LGX = at("logits_x", 193.5, [P, NT, NE])
        FSM = at("ffn_small2", 194, [P, 64])
        RMX, RSM, RRC = FSM[:, 0:4], FSM[:, 4:8], FSM[:, 8:12]
        POSC, POSN, AFFC = FSM[:, 12:16], FSM[:, 16:20], FSM[:, 20:24]
        M8 = FSM[0:NE, 32:40]
        ONEROW = bass.AP(ONES.ap().tensor, ONES.ap().offset, [[ONES.ap().ap[0][0], NE], [0, S]])
        V_NORMED, MERGED = 7, 14
        e_sq, v_sq, g_act, x_mul, s_ada, zeroed = sem("e_sq"), sem("v_sq"), sem("gmlp_act"), sem("x_mul"), sem("ada_scaled"), sem("zeroed")

        def k2_final(dve, head_final, j):
            g = j // 2
            head_final(("k2", j), ("k2ss", j), 8 + j, pcol("k_norm_g_2"), in_order(K2[:, g, j % 2, :], g),
                       lambda x: to_order(x, g))

        def q2_final(dve, head_final, g, j):
            head_final(("q2", g, j), ("q2ss", g, j), 14 + 8 * g + j, QG2, in_order(Q2[:, j, :], g),
                       lambda x: to_order(x, g))

        block = ctx.enter_context(nc.Block())

        @block.sync
        def _(sp):
            sp.dma_start(CE[:, :], c_early).then_inc(s_const, 16)
            for name, rows in COL_ROWS:
                src = a[name]
                flat = src if len(src.shape) == 1 else src[0]
                for j in range(2 if name in ("q_norm", "k_norm") else 1):
                    n = min(flat.shape[0], rows * P)
                    sp.dma_start(ROWS_IN[COL[name]:COL[name] + rows, j * HD1:j * HD1 + n // rows],
                                 flat[0:n].rearrange("(r c) -> r c", r=rows)).then_inc(s_rows, 16)

            def load(n):
                src, _, _ = stream[n]
                if n >= RING:
                    _, kind, i = stream[n - RING]
                    if kind == "W":
                        sp.wait_ge(lo_ready, i + 1)
                    else:
                        sp.wait_ge(ada_step, ada_done(i))
                sp.dma_start(raw3(n, src.shape[1]), src).then_inc(loaded[slot(n)], 16)

            for n in range(N_E - 1):
                if stop < 3 and stream[n][1] == "W" and stream[n][2] > W_V[0][1] + 1:
                    return
                load(n)
                if n == 1:
                    sp.dma_start(CW[:, :], c_wins).then_inc(s_wins, 16)
                    sp.dma_start(GATE_A[:, :], bc(a["a_ada_b_2"], 2 * D, D)).then_inc(s_ga, 16)
            if stop < 4:
                return
            sp.wait_ge(filled, fill_no(("pool", 3)))
            sp.dma_start(GROW[:, :], bc(a["norm_ffn"], 0, D)).then_inc(s_grow, 16)
            sp.dma_start(CL[:, :], c_late).then_inc(s_late, 16)
            sp.dma_start(WR[:, :, :], a["w_router"][0].rearrange("(k p) e -> p k e", p=P)).then_inc(s_wr, 16)
            sp.dma_start(PTOK[:, :, :], a["p"][0, 0].rearrange("(t p) d -> p t d", p=P)).then_inc(s_p, 16)
            load(N_E - 1)
            if stop < 6:
                return

            wg, wu = (a[x][0].rearrange("e (k p) f -> e p k f", p=P) for x in ("w_gate", "w_up"))
            wd = a["w_down"][0].rearrange("e (k p) d -> e p k d", p=P)
            with sp.Fori(0, NE) as e:
                for i in range(SLABS_E):
                    sp.wait_ge(lo_ready, e * SLABS_E + (WE0 + i - RING + 1))
                    if i < 16:
                        w, h, k = (wg, wu)[i // 4 % 2], i // 8, 2 * (i % 4)
                        src = w[e, :, k:k + 2, h * D:(h + 1) * D]
                    else:
                        k = 2 * (i - 16)
                        src = wd[e, :, k:k + 2, :]
                    sp.dma_start(raw3(N_E + i, 2), src).then_inc(loaded[slot(N_E + i)], 16)
            if stop < 7:
                return
            sp.wait_ge(n_xn, 8)
            sp.dma_start(GROW[:, :], bc(a["norm_ple_post"], 0, D)).then_inc(s_grow, 16)
            n_after = N_E + NE * SLABS_E
            for n in range(n_after, len(stream)):
                _, kind, i = stream[n]
                if kind == "W" and i == W_AV[0][0]:
                    sp.wait_ge(d_add, 8 * NE + 8)
                    sp.dma_start(WS_IN[:, :, :], a["a_w_spatial_2"][0].rearrange("g t s -> t g s")).then_inc(s_ws, 16)
                    sp.dma_start(GATE_B[:, :], bc(a["b_ada_b_2"], 2 * D, D)).then_inc(s_gb, 16)
                if kind == "W" and i in W_AU:
                    g = W_AU.index(i)
                    if g >= 2:
                        sp.wait_ge(freed["dve"], fills[("am", g - 2, 1)][2])
                    sp.dma_start(BS[g % 2][:, :], bc(a["a_b_spatial_2"], g * P, P)).then_inc(s_bs[g % 2], 16)
                load(n)
            if stop < 99:
                return
            sp.wait_ge(x_upd, 32)
            sp.dma_start(out[0].rearrange("(t p) d -> p t d", p=P), X[:, :, :]).then_inc(s_store, 16)
            sp.wait_ge(s_store, 16)

        @block.gpsimd
        def _(pool):
            nc.gpsimd.memset(RPB[:, :, :], 0.0).then_inc(s_pad, 1)
            pool.wait_ge(s_pad, 1)
            pool.dma_start(RPB[:, :, WIN:WIN + 31], a["rpb"][0]).then_inc(s_rpb, 16)
            pool.wait_ge(s_rpb, 16)
            for r in range(ROWS):
                pool.dma_start(rpb_wide[r].rearrange("(h k) j -> h (k j)", h=H1),
                               RPB[:, r:r + ROWS, :].rearrange("h k j -> h (k j)")).then_inc(s_rpb, 16)
            pool.wait_ge(s_rpb, 16 * (ROWS + 1))
            for c in range(16):
                pool.dma_start(BIAS[c * ROWS:(c + 1) * ROWS, :, :],
                               bass.AP(rpb_wide.tensor, c, [[H1 * ROWS * 63, ROWS], [63, H1 * ROWS], [1, 48]])
                               ).then_inc(s_bias, 16)

            def ada_block(b, acc):
                for i in range(4 * b, 4 * b + 4):
                    n = n_of["A"][i]
                    prod = raw3(n, 2)
                    done = ada_done(i - 1)
                    pool.wait_ge(loaded[slot(n)], 16 * (n // RING + 1))
                    nc.gpsimd.tensor_tensor(prod, prod, spread(CSIL[:, 2 * (i % 4):2 * (i % 4) + 2], D),
                                            ALU.mult).then_inc(ada_step, 1)
                    pool.wait_ge(ada_step, done + 1)
                    if i % 4 == 0:
                        if b > 0:
                            key = ("ada", b - 1) if ("ada", b - 1) in fills else ("ada", b - 1, 1)
                            pool.wait_ge(filled, fill_no(key))
                        nc.gpsimd.tensor_tensor(acc[:, :], prod[:, 0, :], prod[:, 1, :], ALU.add).then_inc(ada_step, 1)
                    else:
                        nc.gpsimd.tensor_tensor(acc[:, :], acc[:, :], prod[:, 0, :], ALU.add).then_inc(ada_step, 1)
                        pool.wait_ge(ada_step, done + 2)
                        nc.gpsimd.tensor_tensor(acc[:, :], acc[:, :], prod[:, 1, :], ALU.add).then_inc(ada_step, 1)

            pool.wait_ge(s_csil, 1)
            for b in range(3):
                ada_block(b, ACC1)
            if stop < 3:
                return
            pool.wait_ge(filled, fill_no(("v", 3)))
            pool.dma_start(WP[:, :, :], a["w_pool"][0].rearrange("g c d -> c g d")).then_inc(s_wp, 16)
            pool.wait_ge(freed["act"], fills[("in", 3)][2])
            n, wins_ = 0, (W2, W4, W8, W16)
            for g in range(4):
                if g:
                    pool.wait_ge(p_step, n)
                pool.dma_start(CNT[:, :], bc(c_cnt, g * S, S)).then_inc(s_cnt, 16)
                cur = UP[:, g, :]
                lo, hi, reach = 0, S + 16, 1
                for k in range(g + 1):
                    nxt = wins_[k][:, :]
                    if n:
                        pool.wait_ge(p_step, n)
                    if k == 0:
                        lo += 1
                        nc.gpsimd.tensor_tensor(nxt[:, lo:hi], cur[:, lo - 1:hi - 1], cur[:, lo:hi],
                                                ALU.add).then_inc(p_step, 1)
                    else:
                        lo, hi = lo + reach, hi - reach
                        nc.gpsimd.tensor_tensor(nxt[:, lo:hi], cur[:, lo - reach:hi - reach],
                                                cur[:, lo + reach:hi + reach], ALU.add).then_inc(p_step, 1)
                        reach *= 2
                    n += 1
                    cur = nxt
                pool.wait_ge(p_step, n)
                pool.wait_ge(s_cnt, 16 * (g + 1))
                nc.gpsimd.tensor_tensor(DT[:, g, :], cur[:, 8:8 + S], CNT[:, :], ALU.mult).then_inc(p_step, 1)
                n += 1
                pool.wait_ge(p_step, n)
                nc.gpsimd.tensor_tensor(DT[:, g, :], DT[:, g, :], UP[:, g, 8:8 + S],
                                        ALU.subtract).then_inc(p_step, 1)
                n += 1
            if stop < 8:
                return
            pool.wait_ge(d_add, 8 * NE + 8)
            for b in range(3, 8):
                ada_block(b, ACC2)

        POOL_STEPS = 1 + 2 + 3 + 4 + 2 * 4

        @block.tensor
        def _(pe):
            mm = nc.tensor.matmul
            at_fill = [0]

            def begin(key):
                assert order[at_fill[0]] == key, (order[at_fill[0]], key)
                at_fill[0] += 1
                i, _, _, r0 = fills[key]
                if i - r0 >= 8:
                    _, eng, n, _ = fills[order[i - 8]]
                    pe.wait_ge(freed[eng], n)
                return bank(key)

            def norm(k):
                for kc in range(KD):
                    b = begin(("norm", k, kc))
                    for t in range(NT):
                        last = nc.tensor.transpose(b[:, t * P:(t + 1) * P], XN[:, t, kc * P:(kc + 1) * P], ident)
                    last.then_inc(filled, 1)

            def slab_ready(w):
                pe.wait_ge(lo_ready, w + 1)
                return WHI[w % 2], WLO[w % 2]

            def fm_chunk(w, c, key, ah, al):
                hi, lo = slab_ready(w)
                b = begin(key)
                for kc in range(KD):
                    cols = slice(kc * 256 + c * P, kc * 256 + (c + 1) * P)
                    mm(b[:, :], hi[:, cols], ah[:, kc, :], start=(kc == 0), stop=False)
                    mm(b[:, :], hi[:, cols], al[:, kc, :], start=False, stop=False)
                    last = mm(b[:, :], lo[:, cols], ah[:, kc, :], start=False, stop=(kc == KD - 1))
                last.then_inc(filled, 1)

            def tm_unit(ws, keys, ah, al):
                banks = []
                for s in range(2):
                    hi, lo = slab_ready(ws[s])
                    for t in range(NT):
                        if s == 0:
                            banks.append(begin(keys[t]))
                        b = banks[t]
                        for k in range(4):
                            kc = 4 * s + k
                            a_hi, a_lo = ah[:, kc, t * P:(t + 1) * P], al[:, kc, t * P:(t + 1) * P]
                            r = slice(k * 512, (k + 1) * 512)
                            mm(b[:, :], a_hi, hi[:, r], start=(kc == 0), stop=False)
                            mm(b[:, :], a_hi, lo[:, r], start=False, stop=False)
                            last = mm(b[:, :], a_lo, hi[:, r], start=False, stop=(kc == KD - 1))
                        if s == 1:
                            last.then_inc(filled, 1)
                    if s == 0:
                        last.then_inc(half_used, 1)

            def head_squares(key, j, ones_ap):
                pe.wait_ge(h_sq, j + 1)
                b = begin(key)
                mm(b[:, :], ones_ap, SQ[j % 2][:, :], start=True, stop=True).then_inc(filled, 1)

            def ada_cols(b_, acc):
                pe.wait_ge(ada_step, ada_done(4 * b_ + 3))
                b = begin(("ada", b_))
                for c in range(KD):
                    last = mm(b[:, c:c + 1], acc[:, c * P:(c + 1) * P], ONES[:, 0:1], start=True, stop=True)
                last.then_inc(filled, 1)

            def ada_rows(b_, acc):
                pe.wait_ge(ada_step, ada_done(4 * b_ + 3))
                for h in range(2):
                    b = begin(("ada", b_, h))
                    mm(b[:, :], ONES[:, :], acc[:, h * 512:(h + 1) * 512], start=True, stop=True).then_inc(filled, 1)

            pe.wait_ge(s_const, 16)
            pe.wait_ge(s_rows, 16 * (len(COL_ROWS) + 2))
            b = begin(("cols",))
            nc.tensor.transpose(b[:, 0:NCOL], ROWS_IN[0:NCOL, :], ident[0:NCOL, 0:NCOL]).then_inc(filled, 1)
            pe.wait_ge(s_init, 4)
            pe.wait_ge(n_xn, 4)
            norm(0)
            if stop < 2:
                return
            pe.wait_ge(f_lo, 8)
            for j in range(12):
                fm_chunk(W_IN[j // 2], j % 2, ("in", j), AH, AL)
                if j >= 5:
                    head_squares(("inss", j - 1), j - 5, blocks64)
                if j == 5:
                    ada_cols(0, ACC1)
                if j == 9:
                    ada_cols(1, ACC1)
            head_squares(("inss", 11), 7, blocks64)
            tm_unit(W_V[0], [("v", t) for t in range(NT)], AH, AL)
            ada_rows(2, ACC1)
            if stop < 3:
                return

            pe.wait_ge(s_wins, 16)
            pe.wait_ge(freed["dve"], fills[("in", 11)][2])
            pe.wait_ge(freed["act"], fills[("v", 3)][2])
            n_items = len(ITEMS1)
            for j in range(n_items + 2):
                if j < n_items:
                    tr, t, h, kts, n = item1(j)
                    rows = slice((h % 2) * HD1, (h % 2 + 1) * HD1)
                    b = begin(("a1s", j))
                    mm(b[:, 0:n], ident_bf, CW[:, WINC[t]:WINC[t] + n], start=True, stop=False)
                    mm(b[:, 0:n], Q1[rows, h // 2, tr * P:(tr + 1) * P],
                       K1[rows, h // 2, kts[0] * P:kts[0] * P + n], start=False, stop=True).then_inc(filled, 1)
                if 1 <= j <= n_items:
                    _, _, _, kts, n = item1(j - 1)
                    pe.wait_ge(a_exp, j)
                    b = begin(("a1t", j - 1))
                    for i in range(len(kts)):
                        last = nc.tensor.transpose(b[:, i * P:(i + 1) * P], P1[(j - 1) % 2][:, i * P:(i + 1) * P], ident)
                    last.then_inc(filled, 1)
                if j >= 2:
                    _, _, h, kts, n = item1(j - 2)
                    pe.wait_ge(freed["act"], fills[("a1t", j - 2)][2])
                    b = begin(("a1o", j - 2))
                    for i, kt in enumerate(kts):
                        last = mm(b[:, 0:HD1], PT1[j % 2][:, i * P:(i + 1) * P], V1[:, kt, h * HD1:(h + 1) * HD1],
                                  start=(i == 0), stop=(i == len(kts) - 1))
                    last.then_inc(filled, 1)
            pe.wait_ge(s_wp, 16)
            pe.wait_ge(p_step, POOL_STEPS)
            for g in range(4):
                b = begin(("pool", g))
                mm(b[:, :], WP[:, g, :], DT[:, g, :], start=True, stop=True).then_inc(filled, 1)
            pe.wait_ge(freed["dve"], fills[("a1o", n_items - 1)][2])
            for c in range(4):
                b = begin(("ot1", c))
                for t in range(NT):
                    last = nc.tensor.transpose(b[:, t * P:(t + 1) * P], O1[:, t, c * P:(c + 1) * P], ident)
                last.then_inc(filled, 1)
            if stop < 4:
                return
            pe.wait_ge(f_lo, 16)
            for h in range(2):
                tm_unit(W_OUT[h], [("wout", h, t) for t in range(NT)], BH, BL)

            pe.wait_ge(n_xn, 8)
            pe.wait_ge(s_wr, 16)
            for kc in range(KD + 1):
                if kc < KD:
                    b = begin(("norm", 1, kc))
                    for t in range(NT):
                        last = nc.tensor.transpose(b[:, t * P:(t + 1) * P], XN[:, t, kc * P:(kc + 1) * P], ident)
                    last.then_inc(filled, 1)
                if kc == 1:
                    lg = begin(("logits",))
                if kc:
                    pe.wait_ge(freed["act"], fills[("norm", 1, kc - 1)][2])
                    for t in range(NT):
                        last = mm(lg[:, t * NE:(t + 1) * NE], FULL[(kc - 1) % 2][:, t * P:(t + 1) * P], WR[:, kc - 1, :],
                                  start=(kc == 1 and t == 0), stop=(kc == KD), skip_group_check=True)
                        if kc == 1 and t == 0:
                            last.then_inc(filled, 1)
                    last.then_inc(r_used, 1)
            if stop < 5:
                return
            pe.wait_ge(k_step, 5)
            b = begin(("aff_t",))
            for t in range(NT):
                last = nc.tensor.transpose(b[0:NE, t * P:(t + 1) * P], AFF[:, t, 0:NE], ident)
            last.then_inc(filled, 1)
            pe.wait_ge(s_p, 16)
            for c in range(2):
                b = begin(("pt", c))
                for t in range(NT):
                    last = nc.tensor.transpose(b[:, t * P:(t + 1) * P], PTOK[:, t, c * P:(c + 1) * P], ident)
                last.then_inc(filled, 1)
            pe.wait_ge(f_lo, 18)
            hi, lo = slab_ready(W_PROJ)
            for h in range(2):
                for t in range(NT):
                    b = begin(("proj", h, t))
                    for k in range(2):
                        r = slice(k * D + h * 512, k * D + (h + 1) * 512)
                        p_h, p_l = PH[:, k, t * P:(t + 1) * P], PL[:, k, t * P:(t + 1) * P]
                        mm(b[:, :], p_h, hi[:, r], start=(k == 0), stop=False)
                        mm(b[:, :], p_h, lo[:, r], start=False, stop=False)
                        last = mm(b[:, :], p_l, hi[:, r], start=False, stop=(k == 1))
                    last.then_inc(filled, 1)
            pe.wait_ge(k_step, 5 + 16 + 3)
            b = begin(("pos_t",))
            for t in range(NT):
                last = nc.tensor.transpose(b[:, t * NE:(t + 1) * NE], RANK[:, t * P:(t + 1) * P], ident[0:NE, 0:NE])
            last.then_inc(filled, 1)
            if stop < 6:
                return

            def gather():
                for c in range(KD):
                    b = PS[7 - c // 4]
                    for part, src in enumerate((TH, TL)):
                        o = (c % 4) * P + part * CAP
                        for t in range(NT):
                            last = mm(b[:, o:o + CAP], src[:, t, c * P:(c + 1) * P], SEL[:, t, :],
                                      start=(t == 0), stop=(t == NT - 1))
                last.then_inc(m_x, 1)

            def turn(src, b):
                for c in range(8):
                    last = mm(b[:, c * CAP:(c + 1) * CAP], src[:, c * P:(c + 1) * P], stack64, start=True, stop=True)
                return last

            def expert_slab(i, lhs, banks, first, final):
                hi, lo = WHI_E[i % 3], WLO_E[i % 3]
                for k in range(2):
                    for n in range(2):
                        r = slice(k * D + n * 512, k * D + (n + 1) * 512)
                        mm(banks[n][:, :], lhs[k], hi[:, r], start=(first and k == 0), stop=False)
                        last = mm(banks[n][:, :], lhs[k], lo[:, r], start=False, stop=(final and k == 1))
                last.then_inc(e_used, 1)

            def combine(j, base_):
                t, h = j // 2, j % 2
                if j >= 2:
                    pe.wait_ge(d_add, base_ + (j - 1))
                mm(PS[6 + j % 2][:, :], SELT[:, t * P:(t + 1) * P], Y[:, h * 512:(h + 1) * 512],
                   start=True, stop=True).then_inc(m_c, 1)

            pe.sem_inc(e_used, 3)
            pe.wait_ge(freed["act"], COUNT_BEFORE_E["act"])
            pe.wait_ge(freed["dve"], COUNT_BEFORE_E["dve"])
            pe.wait_ge(t_lo, 4)
            pe.wait_ge(zeroed, 3)
            pe.wait_ge(d_sel, 1)
            gather()
            with pe.Fori(0, NE) as e:
                pe.wait_ge(v_xe, e + 1)
                for i in range(16):
                    if i in (0, 4, 8, 12):
                        pe.wait_ge(v_gu, e * 4 + (3 + i // 4))
                    if i == 13:
                        pe.wait_ge(d_add, e * 8 + 8)
                        turn(GS, PS[6])
                        turn(US, PS[7]).then_inc(m_t, 1)
                    pe.wait_ge(lo_ready, e * SLABS_E + (WE0 + i + 1))
                    q = i % 4
                    two = (PS[0], PS[1]) if i // 4 % 2 == 0 else (PS[2], PS[3])
                    expert_slab(i, [XE[:, 2 * q + k, :] for k in range(2)], two, q == 0, q == 3)
                    if i == 2:
                        pe.wait_ge(v_y, e + 1)
                        pe.wait_ge(v_st, e + 1)
                    if 2 <= i < 10:
                        combine(i - 2, e * 8)
                pe.wait_ge(d_lo, e * 2 + 1)
                for q in range(8):
                    if q == 2:
                        pe.wait_ge(v_gu, e * 4 + 8)
                        pe.wait_ge(d_prod, e * 2 + 1)
                        turn(GS, PS[6])
                        turn(US, PS[7]).then_inc(m_t, 1)
                    if q == 4:
                        pe.wait_ge(d_lo, e * 2 + 2)
                    if q == 5:
                        pe.wait_ge(d_sel, e + 2)
                        gather()
                    if q == 7:
                        pe.wait_ge(d_selg, e + 1)
                        pe.wait_ge(v_xe, e + 2)
                        for t in range(NT):
                            last = mm(PS[6][:, t * P:(t + 1) * P], SELG[:, t, :], ident, start=True, stop=True)
                        last.then_inc(m_s, 1)
                    pe.wait_ge(lo_ready, e * SLABS_E + (WE0 + 16 + q + 1))
                    expert_slab(16 + q, [HM[:, 2 * q + k, :] for k in range(2)], (PS[4], PS[5]), q == 0, q == 7)
            pe.wait_ge(v_y, NE + 1)
            pe.wait_ge(v_st, NE + 1)
            for j in range(8):
                combine(j, 8 * NE)
            if stop < 7:
                return

            pe.wait_ge(n_xn, 12)
            norm(2)
            pe.wait_ge(f_lo, 26)
            for h in range(2):
                tm_unit(W_PGATE[h], [("pgate", h, t) for t in range(NT)], AH, AL)
            if stop < 8:
                return

            pe.wait_ge(n_xn, 16)
            norm(3)
            pe.wait_ge(s_ws, 16)
            for i in range(2):
                b = begin(("ws", i))
                for g in range(4):
                    last = nc.tensor.transpose(b[:, g * P:(g + 1) * P], WS_IN[:, 4 * i + g, :], ident)
                last.then_inc(filled, 1)
            pe.wait_ge(f_lo, 34)
            for h in range(4):
                tm_unit(W_AV[h], [("av", h, t) for t in range(NT)], AH, AL)
                if h >= 1:
                    ada_cols(h + 2, ACC2)
            pe.wait_ge(g_small, V_NORMED)
            for g in range(8):
                for c in range(2):
                    b = begin(("am", g, c))
                    e0 = g * 256 + c * P
                    for t in range(NT):
                        last = mm(b[:, t * P:(t + 1) * P], VV[:, t, e0:e0 + P], WST[:, g, :], start=True, stop=True)
                    last.then_inc(filled, 1)
                for c in range(2):
                    fm_chunk(W_AU[g], c, ("au", g, c), AH, AL)
                for c in range(2):
                    fm_chunk(W_AZ[g], c, ("az", g, c), AH, AL)
                if g == 0:
                    ada_cols(6, ACC2)
                if g == 3:
                    ada_rows(7, ACC2)
                if g % 4 == 3:
                    pe.wait_ge(f_lo, 34 + 8 * (g // 4 + 1))
                    for h in range(2):
                        tm_unit(W_AO[g // 4][h], [("ao", g // 4, h, t) for t in range(NT)], BH, BL)
            if stop < 9:
                return

            pe.wait_ge(n_xn, 20)
            norm(4)
            pe.wait_ge(f_lo, 58)
            for j in range(6):
                fm_chunk(W_K[j // 2], j % 2, ("k2", j), AH, AL)
                if j >= 1:
                    head_squares(("k2ss", j - 1), 8 + j - 1, ONES[:, :])
            head_squares(("k2ss", 5), 8 + 5, ONES[:, :])
            for g in range(NG):
                hi, lo = slab_ready(W_VK[g])
                for t in range(NT):
                    b = begin(("v2", g, t))
                    for kc in range(KD):
                        a_hi, a_lo = tile_of(AH[:, kc, :], g, t), tile_of(AL[:, kc, :], g, t)
                        r = slice(kc * 256, (kc + 1) * 256)
                        mm(b[:, 0:256], a_hi, hi[:, r], start=(kc == 0), stop=False)
                        mm(b[:, 0:256], a_hi, lo[:, r], start=False, stop=False)
                        last = mm(b[:, 0:256], a_lo, hi[:, r], start=False, stop=(kc == KD - 1))
                    last.then_inc(filled, 1)
            norm(5)
            pe.wait_ge(f_lo, 66)
            for g in range(NG):
                for j in range(H2):
                    fm_chunk(W_Q[g][j // 2], j % 2, ("q2", g, j), AH, AL)
                    if j >= 1:
                        head_squares(("q2ss", g, j - 1), 14 + 8 * g + j - 1, ONES[:, :])
                head_squares(("q2ss", g, 7), 14 + 8 * g + 7, ONES[:, :])
                pe.wait_ge(freed["dve"], fills[("q2", g, 7)][2])
                pe.wait_ge(freed["act"], fills[("v2", NG - 1, 3)][2])
                n_items, j0 = NT * H2, 32 * (g + 1)
                tag = f"b{g}"
                for j in range(n_items + 2):
                    if j < n_items:
                        t, h, kts, n = item2(g, j)
                        b = begin((tag + "s", j))
                        mm(b[:, 0:n], Q2[:, h, t * P:(t + 1) * P], K2[:, g, h // 4, kts[0] * P:kts[0] * P + n],
                           start=True, stop=True).then_inc(filled, 1)
                    if 1 <= j <= n_items:
                        _, _, kts, n = item2(g, j - 1)
                        pe.wait_ge(a_exp, j0 + j)
                        b = begin((tag + "t", j - 1))
                        for i in range(len(kts)):
                            last = nc.tensor.transpose(b[:, i * P:(i + 1) * P], P2[(j - 1) % 2][:, i * P:(i + 1) * P], ident)
                        last.then_inc(filled, 1)
                    if j >= 2:
                        _, h, kts, n = item2(g, j - 2)
                        pe.wait_ge(freed["act"], fills[(tag + "t", j - 2)][2])
                        b = begin((tag + "o", j - 2))
                        for i, kt in enumerate(kts):
                            last = mm(b[:, 0:P], PT2[j % 2][:, i * P:(i + 1) * P],
                                      V2[:, g, kt, (h // 4) * P:(h // 4 + 1) * P],
                                      start=(i == 0), stop=(i == len(kts) - 1))
                        last.then_inc(filled, 1)
            if stop < 10:
                return

            for g in range(NG):
                for key, src in ((("nm_t", g), NM2), (("l_t", g), L2)):
                    b = begin(key)
                    for t in range(NT):
                        last = nc.tensor.transpose(b[0:H2, t * P:(t + 1) * P], src[:, g, t * H2:(t + 1) * H2], ident)
                    last.then_inc(filled, 1)
            pe.wait_ge(c_step, MERGED)
            for g in range(NG):
                b = begin(("wg", g))
                for t in range(NT):
                    last = nc.tensor.transpose(b[:, t * H2:(t + 1) * H2], LT2[g][:, t * P:(t + 1) * P], ident[0:H2, 0:H2])
                last.then_inc(filled, 1)
            for h in range(H2):
                fm_chunk(W_Z[h // 2], h % 2, ("z", h), AH, AL)
                pe.wait_ge(c_step, MERGED + 12 * (h + 1))
                b = begin(("comb", h))
                for g in range(NG):
                    for t in range(NT):
                        last = mm(tile_of(b[:, :], g, t), O2[g][:, h, t, :], DG[h % 2][:, g * NT + t, :],
                                  start=(g == 0 and t == 0), stop=(g == NG - 1), skip_group_check=True)
                last.then_inc(filled, 1)
            pe.wait_ge(f_lo, 74)
            for h in range(2):
                tm_unit(W_BO[h], [("bo", h, t) for t in range(NT)], BH, BL)

        JUNK = at("junk", 148, [P, D])

        @block.scalar
        def _(act):
            for t in range(NT):
                act.dma_start(X[:, t, :], a["x"][0, t * P:(t + 1) * P, :]).then_inc(s_x, 16)
            split_at, f = [0], [0]

            def split_upto(w_last):
                while split_at[0] <= w_last:
                    w = split_at[0]
                    n = n_of["W"][w]
                    act.wait_ge(loaded[slot(n)], 16 * (n // RING + 1))
                    if w >= 2:
                        act.wait_ge(*used_by[w - 2])
                    nc.scalar.copy(WHI[w % 2][:, :], RAW[slot(n)][:, :]).then_inc(hi_ready, 1)
                    split_at[0] += 1

            def take(key):
                act.wait_ge(filled, fill_no(key))
                return bank(key)

            def stats(k):
                for t in range(NT):
                    nc.scalar.activation(XN[:, t, :], X[:, t, :], ACT.Square, accum_out=SS[:, t:t + 1]).then_inc(n_sq, 1)
                act.wait_ge(n_ms, k + 1)
                nc.scalar.activation(STD, MS, ACT.Sqrt).then_inc(n_sqrt, 1)

            def full(key, out_ap=None, in_ap=None, mul=1.0, add=0.0):
                b = take(key)
                if f[0] >= 2:
                    act.wait_ge(f_lo, f[0] - 1)
                dst = FULL[f[0] % 2][:, :]
                nc.scalar.activation(dst if out_ap is None else out_ap(dst), b[:, :] if in_ap is None else in_ap(b[:, :]),
                                     ACT.Identity, bias=add, scale=mul).then_inc(freed["act"], 1)
                f[0] += 1

            def norm_full(k):
                for kc in range(KD):
                    full(("norm", k, kc), mul=NORM_MUL[k](kc), add=NORM_ADD[k](kc) if k in NORM_ADD else 0.0)

            def head_square(key, j):
                nc.scalar.activation(SQ[j % 2][:, :], take(key)[:, :], ACT.Square).then_inc(h_sq, 1)

            def head_std(key, j, width, reader=None):
                b = take(key)
                if reader is not None:
                    act.wait_ge(freed["dve"], fills[reader][2])
                nc.scalar.activation(FULL[j % 2][:, :], b[:, :], ACT.Sqrt, bias=EPSC, scale=1.0 / width
                                     ).then_inc(freed["act"], 1)

            def attention(tag, n_items, j0, s_buf, p_buf, pt_buf, width, nm, rs):
                for j in range(n_items + 1):
                    if j < n_items:
                        n = width(j)
                        act.wait_ge(a_nm, j0 + j + 1)
                        if j >= 2:
                            act.wait_ge(filled, fill_no((tag + "t", j - 2)))
                            if tag == "a1":
                                act.wait_ge(a_rr, j - 1)
                        nc.scalar.activation(p_buf[j % 2][:, 0:n], s_buf[j % 2][:, 0:n], ACT.Exp, bias=nm(j),
                                             accum_out=rs(j)).then_inc(a_exp, 1)
                    if j >= 1:
                        n = width(j - 1)
                        b = take((tag + "t", j - 1))
                        if j >= 3:
                            act.wait_ge(filled, fill_no((tag + "o", j - 3)))
                        nc.scalar.copy(pt_buf[(j - 1) % 2][:, 0:n], b[:, 0:n]).then_inc(freed["act"], 1)

            act.wait_ge(s_init, 4)
            split_upto(1)
            act.wait_ge(s_x, 64)
            stats(0)
            act.wait_ge(freed["dve"], 1)
            nc.scalar.activation(CSIL, pcol("c_2", 0, KD), ACT.Silu).then_inc(s_csil, 1)
            norm_full(0)
            if stop < 2:
                return
            for j in range(12):
                if j % 2 == 0:
                    split_upto(W_IN[j // 2] + 1)
                if j < 4:
                    b = take(("in", j))
                    nc.scalar.copy(UP[:, j, 8:8 + S].rearrange("p (r c) -> p c r", r=ROWS),
                                   b[:, :].rearrange("p (c r) -> p c r", r=ROWS)).then_inc(freed["act"], 1)
                else:
                    head_square(("in", j), j - 4)
                    if j >= 5:
                        head_std(("inss", j - 1), j - 5, HD1, ("in", j - 3) if j >= 7 else None)
            head_std(("inss", 11), 7, HD1, ("in", 9))
            split_upto(W_V[0][1] + 1)
            for t in range(NT):
                nc.scalar.copy(V1[:, t, :], take(("v", t))[:, :]).then_inc(freed["act"], 1)
            if stop < 3:
                return
            split_upto(W_OUT[0][1])
            attention("a1", len(ITEMS1), 0, S1, P1, PT1, lambda j: item1(j)[4], lambda j: NM[j % 2], lambda j: RS[j % 2])
            for g in range(4):
                full(("pool", g), mul=pcol("pool_scale", g))
            for c in range(4):
                full(("ot1", c), out_ap=lambda x: x.rearrange("p (r c) -> p c r", r=ROWS),
                     in_ap=lambda x: x[:, ::-1].rearrange("p (c r) -> p c r", r=ROWS))
            if stop < 4:
                return
            for h in range(2):
                split_upto(W_OUT[h][1] + 1)
            act.wait_ge(freed["dve"], fills[("wout", 1, 3)][2])
            stats(1)
            for t in range(NT):
                act.wait_ge(n_xn, 4 + t + 1)
                nc.scalar.copy(TH[:, t, :], XN[:, t, :]).then_inc(t_hi, 1)
            for kc in range(KD):
                b = take(("norm", 1, kc))
                if kc >= 2:
                    act.wait_ge(r_used, kc - 1)
                nc.scalar.copy(FULL[kc % 2][:, :], b[:, :]).then_inc(freed["act"], 1)
            if stop < 5:
                return
            act.wait_ge(freed["dve"], fills[("logits",)][2])
            nc.scalar.activation(LGX[:, :, :], LGX[:, :, :], ACT.Exp).then_inc(k_exp, 1)
            act.wait_ge(r_used, KD)
            for c in range(2):
                full(("pt", c))
            for h in range(2):
                for t in range(NT):
                    nc.scalar.copy(E_[:, t, h * 512:(h + 1) * 512], take(("proj", h, t))[:, :]).then_inc(freed["act"], 1)
            for t in range(NT):
                act.wait_ge(freed["act"], fills[("proj", 1, t)][2])
                if t:
                    act.wait_ge(e_sq, t)
                nc.scalar.activation(JUNK[:, :], E_[:, t, :], ACT.Square, accum_out=ESS[:, t:t + 1]).then_inc(e_sq, 1)
            if stop < 6:
                return

            act.wait_ge(*used_by[WE0 - 1])
            act.sem_inc(v_gu, 4)
            act.wait_ge(zeroed, 3)
            act.sem_inc(v_st, 1)
            act.wait_ge(m_x, 1)
            for i in range(2):
                last = nc.scalar.copy(XE[:, 4 * i:4 * i + 4, :], PS[7 - i][:, :].rearrange("p (c j) -> p c j", c=4))
            last.then_inc(v_xe, 1)

            def rows_out(dst, b0):
                nc.scalar.copy(dst[:, 0:512], PS[b0][:, :])
                return nc.scalar.copy(dst[:, 512:D], PS[b0 + 1][:, :])

            with act.Fori(0, NE) as e:
                for i in range(SLABS_E):
                    n = N_E + i
                    act.wait_ge(loaded[slot(n)], e * (16 * SLABS_E // RING) + 16 * (n // RING + 1))
                    act.wait_ge(e_used, e * SLABS_E + (i + 1))
                    nc.scalar.copy(WHI_E[i % 3][:, :], RAW[slot(n)][:, :]).then_inc(hi_ready, 1)
                    if i == 2:
                        rows_out(Y, 4).then_inc(v_y, 1)
                    if i == 6:
                        rows_out(GS, 0).then_inc(v_gu, 1)
                    if i == 10:
                        rows_out(US, 2).then_inc(v_gu, 1)
                    if i == 15:
                        act.wait_ge(m_t, e * 2 + 1)
                        nc.scalar.activation(SQ[0][:, :], PS[6][:, :], ACT.Silu).then_inc(v_silu, 1)
                        rows_out(GS, 0).then_inc(v_gu, 1)
                    if i == 18:
                        rows_out(US, 2).then_inc(v_gu, 1)
                    if i == 20:
                        act.wait_ge(m_t, e * 2 + 2)
                        nc.scalar.activation(SQ[0][:, :], PS[6][:, :], ACT.Silu).then_inc(v_silu, 1)
                act.wait_ge(m_x, e + 2)
                for i in range(2):
                    last = nc.scalar.copy(XE[:, 4 * i:4 * i + 4, :], PS[7 - i][:, :].rearrange("p (c j) -> p c j", c=4))
                last.then_inc(v_xe, 1)
                act.wait_ge(m_s, e + 1)
                nc.scalar.copy(SELT[:, :], PS[6][:, :]).then_inc(v_st, 1)
            act.wait_ge(*used_by[WE0 + NE * SLABS_E - 1])
            rows_out(Y, 4).then_inc(v_y, 1)
            if stop < 7:
                return
            split_at[0] = WE0 + NE * SLABS_E

            split_upto(W_PGATE[0][1])
            act.wait_ge(d_add, 8 * NE + 8)
            stats(2)
            act.wait_ge(k_step, 25)
            nc.scalar.activation(ERSTD, ESS, ACT.Sqrt).then_inc(k_exp, 1)
            norm_full(2)
            for h in range(2):
                split_upto(W_PGATE[h][1] + 1)
                for t in range(NT):
                    i = 4 * h + t
                    b = take(("pgate", h, t))
                    if i >= 2:
                        act.wait_ge(x_upd, i - 1)
                    nc.scalar.activation(SQ[i % 2][:, :], b[:, :], ACT.Sigmoid).then_inc(freed["act"], 1)
            if stop < 8:
                return

            split_upto(W_AV[0][1])
            act.wait_ge(x_upd, 8)
            stats(3)
            norm_full(3)
            n = 0
            for h in range(4):
                split_upto(W_AV[h][1] + 1)
                for t in range(NT):
                    part = VV[:, t, h * 512:(h + 1) * 512]
                    nc.scalar.activation(part, take(("av", h, t))[:, :], ACT.Gelu_apprx_tanh).then_inc(freed["act"], 1)
                    act.wait_ge(freed["act"], fills[("av", h, t)][2])
                    if n >= 2:
                        act.wait_ge(v_sq, n - 1)
                    nc.scalar.activation(SQ[n % 2][:, :], part, ACT.Square, accum_out=SSV[:, 4 * t + h:4 * t + h + 1]
                                         ).then_inc(v_sq, 1)
                    n += 1
            act.wait_ge(g_small, 2)
            nc.scalar.activation(STD, MS, ACT.Sqrt).then_inc(v_sq, 1)
            for g in range(8):
                split_upto(W_AU[g] + 1)
                for c in range(2):
                    b = take(("au", g, c))
                    nc.scalar.activation(b[:, :], b[:, :], ACT.Gelu_apprx_tanh).then_inc(g_act, 1)
                split_upto(W_AZ[g] + 1)
                for c in range(2):
                    b = take(("az", g, c))
                    nc.scalar.activation(b[:, :], b[:, :], ACT.Silu).then_inc(g_act, 1)
                if g % 4 == 3:
                    f[0] += 8
                    for h in range(2):
                        split_upto(W_AO[g // 4][h][1] + 1)
            if stop < 9:
                return

            act.wait_ge(x_upd, 24)
            stats(4)
            norm_full(4)
            for j in range(6):
                if j % 2 == 0:
                    split_upto(W_K[j // 2] + 1)
                head_square(("k2", j), 8 + j)
                if j >= 1:
                    head_std(("k2ss", j - 1), 7 + j, P, ("k2", j - 3) if j >= 3 else None)
            head_std(("k2ss", 5), 13, P, ("k2", 3))
            for g in range(NG):
                split_upto(W_VK[g] + 1)
                for t in range(NT):
                    nc.scalar.copy(V2[:, g, t, :], take(("v2", g, t))[:, 0:256]).then_inc(freed["act"], 1)
            act.wait_ge(freed["dve"], fills[("k2", 5)][2])
            norm_full(5)
            for g in range(NG):
                for j in range(H2):
                    if j % 2 == 0:
                        split_upto(W_Q[g][j // 2] + 1)
                    head_square(("q2", g, j), 14 + 8 * g + j)
                    if j >= 1:
                        head_std(("q2ss", g, j - 1), 13 + 8 * g + j, P, ("q2", g, j - 3) if j >= 3 else None)
                head_std(("q2ss", g, 7), 21 + 8 * g, P, ("q2", g, 5))
                split_upto(W_Q[g][3] + 2)
                attention(f"b{g}", NT * H2, 32 * (g + 1), S2, P2, PT2, lambda j, g=g: item2(g, j)[3],
                          lambda j, g=g: NM2[:, g, j:j + 1], lambda j, g=g: L2[:, g, j:j + 1])
            if stop < 10:
                return
            for g in range(NG):
                act.wait_ge(c_step, 3 + g)
                nc.scalar.activation(NT2[g][:, :], NT2[g][:, :], ACT.Exp).then_inc(c_exp, 1)
            for h in range(H2):
                if h % 2 == 0:
                    split_upto(W_Z[h // 2] + 1)
                b = take(("z", h))
                if h >= 2:
                    act.wait_ge(freed["dve"], fills[("comb", h - 2)][2])
                nc.scalar.activation(SQ[h % 2][:, :], b[:, :], ACT.Silu).then_inc(freed["act"], 1)
            for h in range(2):
                split_upto(min(W_BO[h][1] + 1, len(n_of["W"]) - 1))

        @block.vector
        def _(dve):
            split_at, f = [0], [0]
            tt, ts, stt = nc.vector.tensor_tensor, nc.vector.tensor_scalar, nc.vector.scalar_tensor_tensor

            def split_upto(w_last):
                while split_at[0] <= w_last:
                    w = split_at[0]
                    dve.wait_ge(hi_ready, w + 1)
                    tt(WLO[w % 2][:, :], RAW[slot(n_of["W"][w])][:, :], WHI[w % 2][:, :].bitcast(F32),
                       ALU.subtract).then_inc(lo_ready, 1)
                    split_at[0] += 1

            def take(key):
                dve.wait_ge(filled, fill_no(key))
                return bank(key)

            def norm_x(k):
                dve.wait_ge(n_sq, 4 * (k + 1))
                ts(MS, SS, 1.0 / D, EPS, ALU.mult, ALU.add).then_inc(n_ms, 1)
                dve.wait_ge(n_sqrt, k + 1)
                nc.vector.reciprocal(RSTD, STD).then_inc(n_rstd, 1)
                dve.wait_ge(n_rstd, k + 1)
                if k == 1:
                    dve.wait_ge(s_grow, 16)
                for t in range(NT):
                    if k == 1:
                        stt(out=XN[:, t, :], in0=X[:, t, :], scalar=RSTD[:, t:t + 1], in1=GROW[:, :],
                            op0=ALU.mult, op1=ALU.mult).then_inc(n_xn, 1)
                    else:
                        ts(XN[:, t, :], X[:, t, :], RSTD[:, t:t + 1], None, ALU.mult).then_inc(n_xn, 1)

            def split_full(hi, lo, sem_, value, view=None):
                src = FULL[f[0] % 2][:, :]
                if view is not None:
                    src = view(src)
                dve.wait_ge(sem_, value)
                nc.vector.tensor_copy(hi, src).then_inc(f_hi, 1)
                dve.wait_ge(f_hi, f[0] + 1)
                tt(lo, src, hi.bitcast(F32), ALU.subtract).then_inc(f_lo, 1)
                f[0] += 1

            def norm_split(k, perm=False):
                for kc in range(KD):
                    hi, lo = AH[:, kc, :], AL[:, kc, :]
                    if perm:
                        hi, lo = (x.rearrange("p (c r) -> p r c", r=ROWS) for x in (hi, lo))
                    split_full(hi, lo, freed["act"], fills[("norm", k, kc)][2],
                               (lambda x: x.rearrange("p (r c) -> p r c", r=ROWS)) if perm else None)

            def head_final(key, sskey, j, gain, out_ap, view=lambda x: x):
                r = FULL[j % 2][:, :]
                dve.wait_ge(freed["act"], fills[sskey][2])
                nc.vector.reciprocal(r, r).then_inc(h_rec, 1)
                dve.wait_ge(h_rec, j + 1)
                stt(out=out_ap, in0=view(bank(key)[:, :]), scalar=gain, in1=view(r), op0=ALU.mult, op1=ALU.mult
                    ).then_inc(freed["dve"], 1)

            ADA = {0: ("a_add", "a_ada_b_2", None), 1: ("a_mul", "a_ada_b_2", "a_norm_g_2"),
                   3: ("kv_add", "kv_ada_b_2", None), 4: ("kv_mul", "kv_ada_b_2", "kv_norm_g_2"),
                   5: ("b_add", "b_ada_b_2", None), 6: ("b_mul", "b_ada_b_2", "b_norm_g_2")}

            def ada_out(b_):
                dst, bias, gain = ADA[b_]
                b = take(("ada", b_))
                if gain is None:
                    tt(ADC[dst], b[:, 0:KD], pcol(bias, 0, KD), ALU.add).then_inc(freed["dve"], 1)
                else:
                    tt(ADT, b[:, 0:KD], pcol(bias, KD, KD), ALU.add).then_inc(freed["dve"], 1)
                    dve.wait_ge(freed["dve"], fills[("ada", b_)][2])
                    stt(out=ADC[dst], in0=ADT, scalar=1.0, in1=pcol(gain, 0, KD), op0=ALU.add, op1=ALU.mult
                        ).then_inc(s_ada, 1)

            def ada_gate(b_, gate, s_bias_):
                dve.wait_ge(s_bias_, 16)
                for h in range(2):
                    b = take(("ada", b_, h))
                    part = gate[:, h * 512:(h + 1) * 512]
                    tt(part, b[:, :], part, ALU.add).then_inc(freed["dve"], 1)

            def gated_out(keys, gate):
                for key in keys:
                    h, t = key[-2:]
                    i = x_parts[0]
                    x_parts[0] += 1
                    b = take(key)
                    if i >= 2:
                        dve.wait_ge(x_upd, 8 + i - 1)
                    tt(SQ[i % 2][:, :], b[:, :], gate[:, h * 512:(h + 1) * 512], ALU.mult).then_inc(freed["dve"], 1)
                    dve.wait_ge(freed["dve"], fills[key][2])
                    part = X[:, t, h * 512:(h + 1) * 512]
                    tt(part, part, SQ[i % 2][:, :], ALU.add).then_inc(x_upd, 1)

            x_parts = [0]
            nc.vector.memset(ONES[:, :], 1.0).then_inc(s_init, 1)
            nc.vector.memset(EPSC, EPS).then_inc(s_init, 1)
            nc.vector.memset(UP[:, :, 0:8], 0.0).then_inc(s_init, 1)
            nc.vector.memset(UP[:, :, 8 + S:16 + S], 0.0).then_inc(s_init, 1)
            nc.vector.tensor_copy(PCOL[:, 0:NCOL], take(("cols",))[:, 0:NCOL]).then_inc(freed["dve"], 1)
            dve.wait_ge(freed["dve"], 1)
            ts(QG1, pcol("q_norm"), HD1 ** -0.5, None, ALU.mult).then_inc(s_cols, 1)
            ts(QG2, pcol("b_q_norm_g_2"), P ** -0.5, None, ALU.mult).then_inc(s_cols, 1)
            split_upto(1)
            norm_x(0)
            norm_split(0, perm=True)
            if stop < 2:
                return
            dve.wait_ge(s_cols, 2)

            def in_final(j):
                q = j < 8
                out_ap = Q1[:, j - 4, ::-1] if q else K1[:, j - 8, :]
                head_final(("in", j), ("inss", j), j - 4, QG1 if q else pcol("k_norm"), out_ap)

            for j in range(12):
                if j % 2 == 0:
                    split_upto(W_IN[j // 2] + 1)
                if j >= 5:
                    in_final(j - 1)
                if j == 6:
                    ada_out(0)
                if j == 10:
                    ada_out(1)
            split_upto(W_V[0][1])
            in_final(11)
            ada_gate(2, GATE_A, s_ga)
            if stop < 3:
                return
            split_upto(W_OUT[0][1])

            dve.wait_ge(s_bias, 16 * 16)
            n_items = len(ITEMS1)
            for j in range(n_items + 2):
                if j < n_items:
                    tr, t, h, kts, n = item1(j)
                    b = take(("a1s", j))
                    if j >= 2:
                        dve.wait_ge(a_exp, j - 1)
                    bias = BIAS[:, h * ROWS:(h + 1) * ROWS, BJ[t]:BJ[t] + n // ROWS].rearrange("p k j -> p j k")
                    tt(S1[j % 2][:, 0:n].rearrange("p (j k) -> p j k", k=ROWS),
                       b[:, 0:n].rearrange("p (j k) -> p j k", k=ROWS), bias, ALU.add).then_inc(freed["dve"], 1)
                    dve.wait_ge(freed["dve"], fills[("a1s", j)][2])
                    nc.vector.tensor_reduce(NM[j % 2], S1[j % 2][:, 0:n], AX.X, ALU.max, negate=True).then_inc(a_nm, 1)
                if j >= 2:
                    tr, t, h, kts, n = item1(j - 2)
                    dve.wait_ge(a_exp, j - 1)
                    if j >= 4:
                        dve.wait_ge(freed["dve"], fills[("a1o", j - 4)][2])
                    nc.vector.reciprocal(RR[j % 2], RS[j % 2]).then_inc(a_rr, 1)
                    b = take(("a1o", j - 2))
                    dve.wait_ge(a_rr, j - 1)
                    ts(O1[:, tr, h * HD1:(h + 1) * HD1], b[:, 0:HD1], RR[j % 2], None, ALU.mult).then_inc(freed["dve"], 1)
            for g in range(4):
                split_full(BH[:, g, :], BL[:, g, :], freed["act"], fills[("pool", g)][2])
            dve.wait_ge(filled, fill_no(("ot1", 3)))
            for c in range(4):
                split_full(BH[:, 4 + c, :], BL[:, 4 + c, :], freed["act"], fills[("ot1", c)][2])
            if stop < 4:
                return
            for h in range(2):
                split_upto(W_OUT[h][1] + 1)
                for t in range(NT):
                    part = X[:, t, h * 512:(h + 1) * 512]
                    tt(part, part, take(("wout", h, t))[:, :], ALU.add).then_inc(freed["dve"], 1)

            norm_x(1)
            for t in range(NT):
                dve.wait_ge(t_hi, t + 1)
                tt(TL[:, t, :], XN[:, t, :], TH[:, t, :].bitcast(F32), ALU.subtract).then_inc(t_lo, 1)
            if stop < 5:
                return
            nc.vector.memset(POS[:, :, :], 0.0).then_inc(k_step, 1)
            b = take(("logits",))
            dve.wait_ge(r_used, KD)
            lg = b[:, 0:NT * NE].rearrange("p (t e) -> p t e", e=NE)
            nc.vector.tensor_reduce(RMX, lg, AX.X, ALU.max).then_inc(k_step, 1)
            dve.wait_ge(k_step, 2)
            tt(LGX[:, :, :], lg, spread(RMX, NE), ALU.subtract).then_inc(freed["dve"], 1)
            dve.wait_ge(k_exp, 1)
            nc.vector.tensor_reduce(RSM, LGX[:, :, :], AX.X, ALU.add).then_inc(k_step, 1)
            dve.wait_ge(k_step, 3)
            nc.vector.reciprocal(RRC, RSM).then_inc(k_step, 1)
            dve.wait_ge(k_step, 4)
            tt(AFF[:, :, 0:NE], LGX[:, :, :], spread(RRC, NE), ALU.mult).then_inc(k_step, 1)
            nc.vector.tensor_copy(WORK[0][:, :], take(("aff_t",))[0:NE, :]).then_inc(freed["dve"], 1)
            for c in range(2):
                split_full(PH[:, c, :], PL[:, c, :], freed["act"], fills[("pt", c)][2])
            split_upto(W_PROJ)
            dve.wait_ge(freed["dve"], fills[("aff_t",)][2])
            n = 5
            for r in range(CAP // 8):
                nc.vector.max(M8, WORK[r % 2][:, :]).then_inc(k_step, 1)
                n += 1
                dve.wait_ge(k_step, n)
                nc.vector.match_replace(WORK[(r + 1) % 2][:, :], M8, WORK[r % 2][:, :], -1.0).then_inc(k_step, 1)
                n += 1
                dve.wait_ge(k_step, n)
            ts(MASK[:, :], WORK[0][:, :], 0.0, None, ALU.is_lt).then_inc(k_step, 1)
            dve.wait_ge(k_step, n + 1)
            nc.vector.tensor_tensor_scan(WORK[1][:, :], ONEROW, MASK[:, :], 0.0, ALU.mult, ALU.add).then_inc(k_step, 1)
            dve.wait_ge(k_step, n + 2)
            tt(RANK[:, :], WORK[1][:, :], MASK[:, :], ALU.mult).then_inc(k_step, 1)
            nc.vector.tensor_copy(POS[:, :, 0:NE], take(("pos_t",))[:, 0:NT * NE].rearrange("p (t e) -> p t e", e=NE)
                                  ).then_inc(freed["dve"], 1)
            dve.wait_ge(freed["dve"], fills[("pos_t",)][2])
            if stop < 6:
                return

            def select_inputs():
                for t in range(NT):
                    last = ts(SEL[:, t, :], jmod[:, 0:CAP], POSN[:, t:t + 1], None, ALU.is_equal)
                last.then_inc(d_sel, 1)

            dve.wait_ge(freed["act"], COUNT_BEFORE_E["act"])
            for x in (SELT, PS[4], PS[5]):
                nc.vector.memset(x[:, :], 0.0).then_inc(zeroed, 1)
            nc.vector.tensor_copy(POSN, POS[:, :, 0]).then_inc(d_cur, 1)
            dve.wait_ge(d_cur, 1)
            select_inputs()

            def add_combined(j, base_):
                t, h = j // 2, j % 2
                dve.wait_ge(m_c, base_ + (j + 1))
                part = X[:, t, h * 512:(h + 1) * 512]
                tt(part, part, PS[6 + j % 2][:, :], ALU.add).then_inc(d_add, 1)

            with dve.Fori(0, NE) as e:
                for i in range(SLABS_E):
                    w = i % 3
                    dve.wait_ge(hi_ready, e * SLABS_E + (WE0 + i + 1))
                    tt(WLO_E[w][:, :], RAW[slot(N_E + i)][:, :], WHI_E[w][:, :].bitcast(F32),
                       ALU.subtract).then_inc(lo_ready, 1)
                    if i == 2:
                        nc.vector.tensor_copy(POSC, POS[:, :, e]).then_inc(d_cur, 1)
                        nc.vector.tensor_copy(AFFC, AFF[:, :, e]).then_inc(d_cur, 1)
                        nc.vector.tensor_copy(POSN, POS[:, :, e + 1]).then_inc(d_cur, 1)
                        dve.wait_ge(d_cur, e * 3 + 4)
                        for t in range(NT):
                            last = ts(SELG[:, t, :], jmod, POSC[:, t:t + 1], AFFC[:, t:t + 1],
                                      ALU.is_equal, ALU.mult)
                        last.then_inc(d_selg, 1)
                        select_inputs()
                    if i in (15, 20):
                        half = 0 if i == 15 else 1
                        dve.wait_ge(v_silu, e * 2 + (half + 1))
                        tt(SQ[1][:, :], SQ[0][:, :], PS[7][:, :], ALU.mult).then_inc(d_prod, 1)
                        dve.wait_ge(d_prod, e * 2 + (half + 1))
                        hid = SQ[1][:, :].rearrange("p (c j) -> p c j", j=CAP)
                        hi = HM[:, 8 * half:8 * half + 8, 0:CAP]
                        nc.vector.tensor_copy(hi, hid).then_inc(d_hi, 1)
                        dve.wait_ge(d_hi, e * 2 + (half + 1))
                        tt(HM[:, 8 * half:8 * half + 8, CAP:P], hid, hi.bitcast(F32), ALU.subtract).then_inc(d_lo, 1)
                    if 5 <= i < 13:
                        add_combined(i - 5, e * 8)
            for j in range(8):
                add_combined(j, 8 * NE)
            if stop < 7:
                return
            split_at[0] = WE0 + NE * SLABS_E

            split_upto(W_PGATE[0][1])
            norm_x(2)
            dve.wait_ge(e_sq, 4)
            ts(ESS, ESS, 1.0 / D, EPS, ALU.mult, ALU.add).then_inc(k_step, 1)
            dve.wait_ge(k_exp, 2)
            nc.vector.reciprocal(ERSTD, ERSTD).then_inc(k_step, 1)
            norm_split(2)
            dve.wait_ge(k_step, 26)
            dve.wait_ge(s_grow, 32)
            for t in range(NT):
                stt(out=E_[:, t, :], in0=E_[:, t, :], scalar=ERSTD[:, t:t + 1], in1=GROW[:, :],
                    op0=ALU.mult, op1=ALU.mult).then_inc(k_step, 1)
            for h in range(2):
                split_upto(W_PGATE[h][1] + 1)
                for t in range(NT):
                    i = 4 * h + t
                    dve.wait_ge(k_step, 27 + t)
                    dve.wait_ge(freed["act"], fills[("pgate", h, t)][2])
                    r = slice(h * 512, (h + 1) * 512)
                    tt(SQ[i % 2][:, :], SQ[i % 2][:, :], E_[:, t, r], ALU.mult).then_inc(x_mul, 1)
                    dve.wait_ge(x_mul, i + 1)
                    tt(X[:, t, r], X[:, t, r], SQ[i % 2][:, :], ALU.add).then_inc(x_upd, 1)
            if stop < 8:
                return

            split_upto(W_AV[0][1])
            norm_x(3)
            norm_split(3)
            dve.wait_ge(s_late, 16)
            tril = CL[:, 4 * P:5 * P]
            for i in range(2):
                b = take(("ws", i))
                tt(WST[:, 4 * i:4 * i + 4, :], b[:, :].rearrange("p (g t) -> p g t", g=4), repeat(tril, 4),
                   ALU.mult).then_inc(freed["dve"], 1)
            for h in range(4):
                split_upto(W_AV[h][1] + 1)
                if h >= 1:
                    ada_out(h + 2)
            dve.wait_ge(v_sq, 16)
            nc.vector.tensor_reduce(SS, SSV.rearrange("p (t h) -> p t h", h=4), AX.X, ALU.add).then_inc(g_small, 1)
            dve.wait_ge(g_small, 1)
            ts(MS, SS, 1.0 / (2 * D), EPS, ALU.mult, ALU.add).then_inc(g_small, 1)
            dve.wait_ge(v_sq, 17)
            nc.vector.reciprocal(RSTD, STD).then_inc(g_small, 1)
            dve.wait_ge(g_small, 3)
            for t in range(NT):
                ts(VV[:, t, :], VV[:, t, :], RSTD[:, t:t + 1], None, ALU.mult).then_inc(g_small, 1)
            for g in range(8):
                split_upto(W_AU[g])
                dve.wait_ge(s_bs[g % 2], 16 * (g // 2 + 1))
                for c in range(2):
                    b = take(("am", g, c))
                    if g:
                        dve.wait_ge(freed["dve"], fills[("az", g - 1, c)][2])
                        if g == 4 and c == 0:
                            dve.wait_ge(x_upd, 16)
                    elif c == 0:
                        dve.wait_ge(g_small, V_NORMED)
                    stt(out=SQ[c][:, :].rearrange("p (n t) -> p n t", n=NT), in0=b[:, :].rearrange("p (n t) -> p n t", n=NT),
                        scalar=pcol("a_sgu_g_2", 2 * g + c), in1=repeat(BS[g % 2][:, :], NT), op0=ALU.mult, op1=ALU.add
                        ).then_inc(freed["dve"], 1)
                split_upto(W_AU[g] + 1)
                for c in range(2):
                    dve.wait_ge(g_act, 4 * g + c + 1)
                    dve.wait_ge(freed["dve"], fills[("am", g, c)][2])
                    tt(SQ[c][:, :], SQ[c][:, :], bank(("au", g, c))[:, :], ALU.mult).then_inc(freed["dve"], 1)
                split_upto(W_AZ[g] + 1)
                for c in range(2):
                    dve.wait_ge(g_act, 4 * g + 2 + c + 1)
                    dve.wait_ge(freed["dve"], fills[("au", g, c)][2])
                    if f[0] >= 2:
                        dve.wait_ge(f_lo, f[0] - 1)
                    tt(FULL[f[0] % 2][:, :], SQ[c][:, :], bank(("az", g, c))[:, :], ALU.mult).then_inc(freed["dve"], 1)
                    kc = (2 * g + c) % KD
                    split_full(BH[:, kc, :], BL[:, kc, :], freed["dve"], fills[("az", g, c)][2])
                if g == 0:
                    ada_out(6)
                if g == 3:
                    ada_gate(7, GATE_B, s_gb)
                if g % 4 == 3:
                    for h in range(2):
                        split_upto(W_AO[g // 4][h][1] + 1)
                        dve.wait_ge(freed["dve"], fills[("az", g, 1)][2])
                        gated_out([("ao", g // 4, h, t) for t in range(NT)], GATE_A)
            if stop < 9:
                return

            norm_x(4)
            norm_split(4)
            for j in range(6):
                if j % 2 == 0:
                    split_upto(W_K[j // 2] + 1)
                if j >= 1:
                    k2_final(dve, head_final, j - 1)
            split_upto(W_VK[0] + 1)
            k2_final(dve, head_final, 5)
            for g in range(1, NG):
                split_upto(W_VK[g] + 1)
            norm_split(5)
            for g in range(NG):
                for j in range(H2):
                    if j % 2 == 0:
                        split_upto(W_Q[g][j // 2] + 1)
                    if j >= 1:
                        q2_final(dve, head_final, g, j - 1)
                q2_final(dve, head_final, g, 7)
                split_upto(W_Q[g][3] + 2)
                dve.wait_ge(freed["dve"], fills[("q2", g, 7)][2])
                dist = (CL[:, 0:2 * P], CL[:, 2 * P:3 * P], CL[:, 3 * P:4 * P])[g]
                n_items, j0, tag = NT * H2, 32 * (g + 1), f"b{g}"
                for j in range(n_items + 2):
                    if j < n_items:
                        t, h, kts, n = item2(g, j)
                        b = take((tag + "s", j))
                        if j >= 2:
                            dve.wait_ge(a_exp, j0 + j - 1)
                        d = dist[:, P:2 * P] if g == 0 and n == P else dist[:, 0:n]
                        stt(out=S2[j % 2][:, 0:n], in0=d, scalar=-slopes[g * H2 + h], in1=b[:, 0:n],
                            op0=ALU.mult, op1=ALU.add).then_inc(freed["dve"], 1)
                        dve.wait_ge(freed["dve"], fills[(tag + "s", j)][2])
                        nc.vector.tensor_reduce(NM2[:, g, j:j + 1], S2[j % 2][:, 0:n], AX.X, ALU.max, negate=True
                                                ).then_inc(a_nm, 1)
                    if j >= 2:
                        t, h, _, _ = item2(g, j - 2)
                        nc.vector.tensor_copy(O2[g][:, h, t, :], take((tag + "o", j - 2))[:, 0:P]).then_inc(freed["dve"], 1)
            if stop < 10:
                return
            for g in range(NG):
                for key, dst in ((("nm_t", g), NT2), (("l_t", g), LT2)):
                    nc.vector.tensor_copy(to_order(dst[g][:, :], g), in_order(take(key)[0:H2, :], g)).then_inc(freed["dve"], 1)
            dve.wait_ge(freed["dve"], fills[("l_t", NG - 1)][2])
            tt(MIN2[:, :], NT2[0][:, :], NT2[1][:, :], ALU.min).then_inc(c_step, 1)
            dve.wait_ge(c_step, 1)
            tt(MIN2[:, :], MIN2[:, :], NT2[2][:, :], ALU.min).then_inc(c_step, 1)
            dve.wait_ge(c_step, 2)
            for g in range(NG):
                tt(NT2[g][:, :], MIN2[:, :], NT2[g][:, :], ALU.subtract).then_inc(c_step, 1)
            for g in range(NG):
                dve.wait_ge(c_exp, g + 1)
                tt(LT2[g][:, :], LT2[g][:, :], NT2[g][:, :], ALU.mult).then_inc(c_step, 1)
            dve.wait_ge(c_step, 8)
            tt(MIN2[:, :], LT2[0][:, :], LT2[1][:, :], ALU.add).then_inc(c_step, 1)
            dve.wait_ge(c_step, 9)
            tt(MIN2[:, :], MIN2[:, :], LT2[2][:, :], ALU.add).then_inc(c_step, 1)
            dve.wait_ge(c_step, 10)
            nc.vector.reciprocal(MIN2[:, :], MIN2[:, :]).then_inc(c_step, 1)
            dve.wait_ge(c_step, 11)
            for g in range(NG):
                tt(in_order(LT2[g][:, :], g), to_order(NT2[g][:, :], g), to_order(MIN2[:, :], g), ALU.mult).then_inc(c_step, 1)
            for g in range(NG):
                nc.vector.tensor_copy(NM2[:, g, :], take(("wg", g))[:, 0:NT * H2]).then_inc(freed["dve"], 1)
            dve.wait_ge(freed["dve"], fills[("wg", NG - 1)][2])

            def diagonals(h):
                for g in range(NG):
                    for t in range(NT):
                        ts(DG[h % 2][:, g * NT + t, :], ident, NM2[:, g, t * H2 + h:t * H2 + h + 1], None,
                           ALU.mult).then_inc(c_step, 1)

            diagonals(0)
            for h in range(H2):
                if h % 2 == 0:
                    split_upto(W_Z[h // 2] + 1)
                if h + 1 < H2:
                    if h >= 1:
                        dve.wait_ge(filled, fill_no(("comb", h - 1)))
                    diagonals(h + 1)
                b = take(("comb", h))
                dve.wait_ge(freed["act"], fills[("z", h)][2])
                dve.wait_ge(f_lo, f[0] - 1)
                tt(FULL[f[0] % 2][:, :], SQ[h % 2][:, :], b[:, :], ALU.mult).then_inc(freed["dve"], 1)
                split_full(BH[:, h, :], BL[:, h, :], freed["dve"], fills[("comb", h)][2])
            for h in range(2):
                split_upto(min(W_BO[h][1] + 1, len(n_of["W"]) - 1))
                gated_out([("bo", h, t) for t in range(NT)], GATE_B)


_OUTS = [((1, S, D), "float32")]


def kernel(**inputs):
    import numpy as _np
    import concourse.bacc as _bacc
    from concourse import mybir as _mybir
    from concourse.bass_utils import run_bass_kernel_spmd as _run

    nc = _bacc.Bacc("TRN2", target_bir_lowering=False, num_devices=1)
    arrays, args = {}, {}
    for name in inputs:
        x = _np.ascontiguousarray(inputs[name])
        arrays[f"in_{name}"] = x
        args[name] = nc.dram_tensor(f"in_{name}", x.shape, _mybir.dt.from_np(x.dtype), kind="ExternalInput").ap()
    shape, dtype = _OUTS[0]
    out = nc.dram_tensor("out_0", shape, _mybir.dt.from_np(_np.dtype(dtype)), kind="ExternalOutput").ap()
    bass_kernel(nc, args, out)
    r = _run(nc, [arrays], core_ids=[0])
    return r.results[0]["out_0"]
```

```python
from contextlib import ExitStack

import numpy as np

import concourse.bass as bass
from concourse import mybir

P = 128
D = 1024
KD = D // P
S = 512
NT = S // P
HD1, H1 = 64, 8
ROWS, COLS = 8, 64
WIN = 16
NE, CAP, F = 16, 64, 2048
H2, NG, KV2 = 8, 3, 2
EPS = 1e-6
NEG = -1e30
RING = 4
SLAB = 2048
SLABS_E = 24

F32, F32R, BF16 = mybir.dt.float32, mybir.dt.float32r, mybir.dt.bfloat16
ALU = mybir.AluOpType
ACT = mybir.ActivationFunctionType
AX = mybir.AxisListType

COL_ROWS = (("norm_mix", KD), ("norm_ple", KD), ("a_norm_g_2", KD), ("kv_norm_g_2", KD),
            ("b_norm_g_2", KD), ("pool_scale", 4), ("a_sgu_g_2", 16), ("a_ada_b_2", 16),
            ("kv_ada_b_2", 16), ("b_ada_b_2", 16), ("q_norm", 1), ("k_norm", 1),
            ("b_q_norm_g_2", 1), ("k_norm_g_2", 1), ("c_2", KD))
COL = {}
_n = 0
for _name, _rows in COL_ROWS:
    COL[_name] = _n
    _n += _rows
NCOL = _n


def grid_constants():
    i = np.arange(P)
    ident = np.eye(P, dtype=np.float32)
    blocks = (i[:, None] // HD1 == i[None, :] // HD1).astype(np.float32)
    jmod = np.broadcast_to((i % CAP + 1).astype(np.float32), (P, P))
    stack = (i[:, None] % CAP == np.arange(CAP)[None, :]).astype(np.float32)
    tril = (i[:, None] <= i[None, :]).astype(np.float32)
    far = 1e30
    dq0 = np.concatenate([P + i[:, None] - i[None, :], i[:, None] - i[None, :]], axis=1)
    d0 = np.where((dq0 >= 0) & (dq0 <= 128), dq0, far).astype(np.float32)
    dq = i[:, None] - i[None, :]
    d1 = np.where(dq >= 0, 4.0 * dq, far).astype(np.float32)
    d2 = np.where((dq % 4 == 0) & (dq >= 0), 4.0 * dq, far).astype(np.float32)
    early = np.concatenate([ident, blocks, jmod, stack], axis=1)
    late = np.concatenate([d0, d1, d2, tril], axis=1)

    def window(t, kts):
        c = 16 * t + 15 - i // ROWS
        start = np.clip(c - WIN // 2, 0, COLS - WIN)
        kc = (np.concatenate([16 * k + np.arange(16) for k in kts]))
        ok = (kc[None, :] >= start[:, None]) & (kc[None, :] < start[:, None] + WIN)
        return np.repeat(np.where(ok, 0.0, NEG), ROWS, axis=1)
    wins = np.concatenate([window(1, (0, 1, 2)), window(0, (0, 1)), window(3, (2, 3)), ident], axis=1)
    t = np.arange(S)
    cnt = []
    for w in (2, 4, 8, 16):
        lo = np.clip(t - w // 2, 0, S - 1)
        hi = np.clip(t + (w - w // 2) - 1, 0, S - 1)
        cnt.append(1.0 / (hi - lo + 1))
    return early, late, wins, np.stack(cnt).astype(np.float32)



def bass_kernel(nc, a, out):
    early, late, wins, invcnt = grid_constants()
    c_early = nc.inline_tensor(early, name="c_early").ap()
    c_late = nc.inline_tensor(late, name="c_late").ap()
    c_wins = nc.inline_tensor(wins.astype(mybir.dt.np(BF16)), name="c_wins").ap()
    c_cnt = nc.inline_tensor(invcnt, name="c_cnt").ap()
    rpb_wide = nc.dram_tensor("rpb_wide", (ROWS, H1 * ROWS, 63), F32, kind="Internal").ap()

    with ExitStack() as ctx:
        base = (nc.sbuf_base + 31) // 32 * 32

        def at(name, kb, shape, dt=F32):
            return nc.alloc_sbuf_tensor_at(name, shape, dt, offset=base + int(kb * 1024))

        X = at("x_res", 0, [P, NT, D])
        RAW = [at(f"raw{i}", 16 + 8 * i, [P, SLAB]) for i in range(RING)]
        WHI = [at(f"w_hi{i}", 48 + 8 * i, [P, SLAB], F32R) for i in range(2)]
        WLO = [at(f"w_lo{i}", 64 + 8 * i, [P, SLAB], F32R) for i in range(2)]
        AH = at("act_hi", 80, [P, KD, S], F32R)
        AL = at("act_lo", 96, [P, KD, S], F32R)
        BH = at("mix_hi", 112, [P, KD, S], F32R)
        BL = at("mix_lo", 128, [P, KD, S], F32R)
        WHI_E = WHI + [at("w_hi2", 172, [P, SLAB], F32R)]
        WLO_E = WLO + [at("w_lo2", 180, [P, SLAB], F32R)]
        _bh, _e, _q2 = (at(f"x_norm{k}", k, [P, NT, D]) for k in (112, 156, 176))
        XNORM = (_bh, _e, _bh, _bh, _q2, _q2)
        FULL = [at(f"full{i}", 144 + 2 * i, [P, S]) for i in range(2)]
        SQ = [at(f"square{i}", 148 + 2 * i, [P, S]) for i in range(2)]
        ROWS_IN = at("param_rows", 140, [P, P])
        UP = at("u_padded", 152, [P, 4, S + 16])
        Q1 = at("q1", 160.5, [P, 4, S])
        K1 = at("k1", 168.5, [P, 4, S])
        V1 = at("v1", 176.5, [P, NT, 512])
        BIAS = at("bias_master", 184.5, [P, H1 * ROWS, 48])
        RPB = at("rpb_padded", 132, [H1, 15, 63])
        ACC1 = at("ada_acc1", 136, [P, D])
        W2 = at("win2", 80, [P, S + 16])
        W4 = at("win4", 82.5, [P, S + 16])
        W8 = at("win8", 85, [P, S + 16])
        W16 = at("win16", 87.5, [P, S + 16])
        DT = at("pool_d", 90, [P, 4, S])
        WP = at("w_pool_sb", 98, [P, 4, P])
        CNT = at("cnt_row", 100, [P, 512])
        S1 = [at(f"s1_{i}", 102 + 1.5 * i, [P, 384]) for i in range(2)]
        P1 = [at(f"p1_{i}", 105 + 1.5 * i, [P, 384]) for i in range(2)]
        PT1 = [at(f"pt1_{i}", 108 + 1.5 * i, [P, 384]) for i in range(2)]
        O1 = at("o1", 112 + 8, [P, NT, 512])
        TH = at("tok_hi", 80, [P, NT, D], F32R)
        TL = at("tok_lo", 96, [P, NT, D], F32R)
        GS = at("gate_rows", 112, [P, D])
        US = at("up_rows", 116, [P, D])
        XE = at("chosen", 120, [P, KD, P], F32R)
        HM = at("hidden", 124, [P, 2 * KD, P], F32R)
        Y = at("expert_out", 132, [P, D])
        SELG = at("sel_gated", 136, [P, NT, P])
        SELT = at("sel_gated_t", 138, [P, S])
        SEL = at("sel", 140, [P, NT, 3 * CAP], F32R)
        XG = at("chosen_rows", 144, [P, D])
        GROW = at("gain_row", 152, [P, D])
        E_ = at("ple_e", 156, [P, NT, D])
        PH = at("p_hi", 172, [P, 2, S], F32R)
        PL = at("p_lo", 176, [P, 2, S], F32R)
        PTOK = at("p_tok", 180, [P, NT, 256])
        WORK = [at(f"topk_work{i}", 184 + 2 * i, [NE, S]) for i in range(2)]
        MASK = at("topk_mask", 188, [NE, S])
        RANK = at("topk_rank", 190, [NE, S])
        WR = at("w_router_sb", 192, [P, KD, NE])
        AFF = at("affinity", 192.5, [P, NT, NE + 1])
        POS = at("position", 193, [P, NT, NE + 1])
        VV = at("v_rows", 152, [P, NT, 2 * D])
        WST = at("w_spatial_t", 184, [P, 8, P])
        WS_IN = at("w_spatial_in", 128, [P, 8, P])
        ACC2 = at("ada_acc2", 188, [P, D])
        GATE_B = at("gate_b", 192, [P, D])
        BS = [at(f"b_spatial{i}", 196 + 0.5 * i, [P, P]) for i in range(2)]
        K2 = at("k2", 152, [P, NG, KV2, S])
        V2 = at("v2", 164, [P, NG, NT, KV2 * P])
        Q2 = at("q2", 176, [P, H2, S])
        O2 = [at("o2_0", 112, [P, H2, NT, P]), at("o2_1", 128, [P, H2, NT, P]), at("o2_2", 176, [P, H2, NT, P])]
        NM2 = at("negmax2", 196, [P, NG, NT * H2])
        L2 = at("rowsum2", 196.375, [P, NG, NT * H2])
        NT2 = [at(f"negmax2_t{g}", 152 + 2 * g, [H2, S]) for g in range(NG)]
        LT2 = [at(f"rowsum2_t{g}", 158 + 2 * g, [H2, S]) for g in range(NG)]
        DG = [at(f"diag{i}", 164 + 6 * i, [P, NG * NT, P]) for i in range(2)]
        S2 = [at(f"s2_{i}", 144 + i, [P, 256]) for i in range(2)]
        P2 = [at(f"p2_{i}", 146 + i, [P, 256]) for i in range(2)]
        PT2 = [at(f"pt2_{i}", 148 + i, [P, 256]) for i in range(2)]
        MIN2 = at("min2", 144, [H2, S])
        GATE_A = at("gate_a", 197, [P, D])
        CE = at("const_early", 201, [P, 3 * P + CAP])
        CL = at("const_late", 202.75, [P, 5 * P])
        CW = at("const_wins", 202.75, [P, 896 + P], BF16)
        PCOL = at("param_cols", 205.25, [P, P])
        ONES = at("ones", 205.75, [P, P])
        ST = at("stats", 206.25, [P, 160])
        ident, blocks64, jmod = CE[:, 0:P], CE[:, P:2 * P], CE[:, 2 * P:3 * P]
        stack64 = CE[:, 3 * P:3 * P + CAP]
        ident_bf = CW[:, 896:896 + P]

        def st(i, n=1):
            return ST[:, i:i + n]
        SS, MS, STD, RSTD = st(0, 4), st(4, 4), st(8, 4), st(12, 4)
        QG1, KG1, QG2, KG2 = st(16), st(17), st(18), st(19)
        CSIL, CEXP = st(20, 8), st(28, 8)
        NM = [st(36), st(37)]
        RS = [st(38), st(39)]
        RR = [st(40), st(41)]
        EPSC = st(42)
        ESS, ERSTD = st(44, 4), st(48, 4)
        ADC = {k: st(56 + 8 * i, 8) for i, k in enumerate(("a_add", "a_mul", "kv_add", "kv_mul", "b_add", "b_mul"))}
        ADT = st(104, 8)
        SSV = st(112, 16)

        def pcol(name, k=0, n=1):
            return PCOL[:, COL[name] + k:COL[name] + k + n]

        NORM_MUL = {0: lambda k: pcol("norm_mix", k), 2: lambda k: pcol("norm_ple", k),
                    3: lambda k: ADC["a_mul"][:, k:k + 1], 4: lambda k: ADC["kv_mul"][:, k:k + 1],
                    5: lambda k: ADC["b_mul"][:, k:k + 1]}
        NORM_ADD = {3: lambda k: ADC["a_add"][:, k:k + 1], 4: lambda k: ADC["kv_add"][:, k:k + 1],
                    5: lambda k: ADC["b_add"][:, k:k + 1]}

        def bc(ap, off, n):
            return bass.AP(ap.tensor, ap.offset + off, [[0, P], [1, n]])

        def spread(ap, n):
            return bass.AP(ap.tensor, ap.offset, [list(ap.ap[0]), list(ap.ap[1]), [0, n]])

        def repeat(ap, n):
            return bass.AP(ap.tensor, ap.offset, [list(ap.ap[0]), [0, n], list(ap.ap[1])])

        def ada_done(i):
            return 11 * (i // 4) + 3 * (i % 4) + 2 if i >= 0 else 0

        stream, n_of, before = [], {"W": [], "A": []}, {}

        def slab(kind, src):
            stream.append((src, kind, len(n_of[kind])))
            n_of[kind].append(len(stream) - 1)
            return len(n_of[kind]) - 1

        def fm_src(w, c0):
            return w.rearrange("(k p) n -> p k n", p=P)[:, :, c0:c0 + 256]

        def tm_src(w, k0, c0):
            return w.rearrange("(k p) n -> p k n", p=P)[:, k0:k0 + 4, c0:c0 + 512]

        def wide_src(w, k0, c0):
            return w.rearrange("(k p) n -> p k n", p=P)[:, k0:k0 + 2, c0:c0 + D]

        ada_src = [wide_src(w, k, b * D)
                   for w, nb in ((a["a_ada_w_2"][0], 3), (a["kv_ada_w_2"], 2), (a["b_ada_w_2"][0], 3))
                   for b in range(nb) for k in range(0, KD, 2)]

        def ada_slabs(n):
            for _ in range(n):
                if len(n_of["A"]) < len(ada_src):
                    slab("A", ada_src[len(n_of["A"])])

        def tm_slabs(w, k0=0, cols=2, c0=0):
            return [[slab("W", tm_src(w, k0 + 4 * s, c0 + 512 * h)) for s in range(2)] for h in range(cols)]

        w_in, w_a, w_b = a["w_in"][0], a["a_w_in_2"][0], a["b_w_in_2"][0]
        W_IN = []
        for i in range(6):
            W_IN.append(slab("W", fm_src(w_in, 256 * i)))
            ada_slabs(1 if 1 <= i <= 4 else 0)
        W_V = tm_slabs(w_in, 0, 1, 1536)
        W_OUT = tm_slabs(a["w_out"][0], 0, 1)
        ada_slabs(8)
        W_OUT += tm_slabs(a["w_out"][0], 0, 1, 512)
        W_PROJ = slab("W", wide_src(a["w_ple_proj"][0], 0, 0))
        N_E, WE0 = len(stream), len(n_of["W"])
        for _ in range(NE * SLABS_E):
            slab("W", None)
        W_PGATE = tm_slabs(a["w_ple_gate"][0])
        W_AV = []
        for h in range(4):
            W_AV.append([])
            for i in range(2):
                W_AV[h].append(slab("W", tm_src(w_a, 4 * i, 2048 + 512 * h)))
                ada_slabs(1)
        W_AU, W_AZ, W_AO = [], [], []
        for hh in range(2):
            for g in range(4 * hh, 4 * hh + 4):
                W_AU.append(slab("W", fm_src(w_a, 256 * g)))
                ada_slabs(1)
                W_AZ.append(slab("W", fm_src(w_a, 4096 + 256 * g)))
                if g < 4:
                    ada_slabs(1)
            W_AO.append(tm_slabs(a["a_w_out_2"][0], 8 * hh))
        assert len(n_of["A"]) == len(ada_src)
        W_K = [slab("W", fm_src(a["w_kv_2"], 256 * g)) for g in range(NG)]
        W_VK = [slab("W", fm_src(a["w_kv_2"], 768 + 256 * g)) for g in range(NG)]
        W_Q = [[slab("W", fm_src(w_b, 1024 * g + 256 * i)) for i in range(4)] for g in range(NG)]
        W_Z = [slab("W", fm_src(w_b, 3072 + 256 * i)) for i in range(4)]
        W_BO = tm_slabs(a["b_w_out_2"][0])

        order, fills, count = [], {}, {"act": 0, "dve": 0}
        ring0 = [0]

        def note(key, eng):
            count[eng] += 1
            fills[key] = (len(order), eng, count[eng], ring0[0])
            order.append(key)

        def note_norm(k):
            for kc in range(KD):
                note(("norm", k, kc), "act")
            if k == 1:
                note(("logits",), "dve")

        def note_attn(tag, n):
            for j in range(n + 3):
                if j < n:
                    note((tag + "s", j), "dve")
                if 2 <= j < n + 2:
                    note((tag + "t", j - 2), "act")
                if j >= 3:
                    note((tag + "o", j - 3), "dve")
                if tag == "a1" and j == 12:
                    note(("ada", 1), "dve")

        note(("cols",), "dve")
        note_norm(0)
        for j in range(12):
            note(("in", j), "act" if j < 4 else "dve")
            if j >= 5:
                note(("inss", j - 1), "act")
            if j == 9:
                note(("ada", 0), "dve")
        note(("inss", 11), "act")
        for t in range(NT):
            note(("v", t), "act")
        ITEMS1 = [(t, h) for t in range(NT) for h in range(H1)]
        note_attn("a1", len(ITEMS1))
        note(("ada", 2, 0), "dve")
        note(("ada", 2, 1), "dve")
        for g in range(4):
            note(("pool", g), "act")
        for c in range(4):
            note(("ot1", c), "act")
        for h in range(2):
            for t in range(NT):
                note(("wout", h, t), "dve")
        note_norm(1)
        note(("aff_t",), "dve")
        for c in range(2):
            note(("pt", c), "act")
        for h in range(2):
            for t in range(NT):
                note(("proj", h, t), "act")
        note(("pos_t",), "dve")
        N_BEFORE_E, ring0[0] = len(order), len(order)
        COUNT_BEFORE_E = dict(count)
        note_norm(2)
        for h in range(2):
            for t in range(NT):
                note(("pgate", h, t), "act")
        note_norm(3)
        for i in range(2):
            note(("ws", i), "dve")
        for h in range(4):
            for t in range(NT):
                note(("av", h, t), "act")
            if h == 2:
                note(("ada", 3), "dve")
        for g in range(8):
            for c in range(2):
                note(("au", g, c), "dve")
            for c in range(2):
                note(("az", g, c), "act")
            for c in range(2):
                note(("am", g, c), "dve")
            if g in (0, 2, 4):
                note(("ada", 4 + g // 2), "dve")
            if g == 7:
                note(("ada", 7, 0), "dve")
                note(("ada", 7, 1), "dve")
            if g % 4 == 3:
                for h in range(2):
                    for t in range(NT):
                        note(("ao", g // 4, h, t), "dve")
        note_norm(4)
        for j in range(6):
            note(("k2", j), "dve")
            if j >= 1:
                note(("k2ss", j - 1), "act")
        note(("k2ss", 5), "act")
        for g in range(NG):
            for t in range(NT):
                note(("v2", g, t), "act")
        note_norm(5)
        for g in range(NG):
            for j in range(H2):
                note(("q2", g, j), "dve")
                if j >= 1:
                    note(("q2ss", g, j - 1), "act")
            note(("q2ss", g, H2 - 1), "act")
            note_attn(f"b{g}", NT * H2)
        for g in range(NG):
            note(("nm_t", g), "dve")
            note(("l_t", g), "dve")
        note(("z", 0), "act")
        note(("z", 1), "act")
        for g in range(NG):
            note(("wg", g), "dve")
        for h in range(H2):
            note(("comb", h), "dve")
            if h + 2 < H2:
                note(("z", h + 2), "act")
        for h in range(2):
            for t in range(NT):
                note(("bo", h, t), "dve")

        def bank(key):
            i, _, _, r0 = fills[key]
            return PS[(i - r0) % 8]

        def fill_no(key):
            return fills[key][0] + 1

        PS = [ctx.enter_context(nc.psum_tensor(f"bank{i}", [P, 512], F32)) for i in range(8)]

        def sem(name):
            return ctx.enter_context(nc.semaphore(name))

        loaded = [sem(f"slab_loaded{i}") for i in range(RING)]
        hi_ready, lo_ready = sem("w_hi_ready"), sem("w_lo_ready")
        half_used, e_used = sem("first_slab_used"), sem("expert_slab_used")
        filled = sem("bank_filled")
        freed = {"act": sem("bank_read_by_act"), "dve": sem("bank_read_by_dve")}
        ada_step = sem("ada_step")
        s_const, s_rows, s_x = sem("consts_loaded"), sem("rows_loaded"), sem("x_loaded")
        s_wins, s_ga, s_wp, s_cnt = sem("windows_loaded"), sem("gate_a_bias"), sem("w_pool_loaded"), sem("counts_loaded")
        s_rpb, s_pad, s_bias = sem("rpb_loaded"), sem("rpb_zeroed"), sem("bias_loaded")
        s_init, s_cols, s_csil, s_cexp = sem("dve_init"), sem("cols_ready"), sem("c_silu"), sem("c_exp")
        n_sq, n_ms, n_sqrt, n_rstd, n_xn = (sem(x) for x in ("norm_sq", "norm_ms", "norm_sqrt", "norm_rstd", "norm_x"))
        f_hi, f_lo = sem("split_hi"), sem("split_lo")
        h_sq, h_rec = sem("head_sq"), sem("head_rec")
        p_step = sem("pool_step")
        a_nm, a_exp, a_rr = sem("neg_max"), sem("exp_done"), sem("row_rec")
        s_grow, s_late, s_wr, s_p = sem("gain_row"), sem("late_loaded"), sem("router_loaded"), sem("p_loaded")
        t_hi, t_lo = sem("tok_hi"), sem("tok_lo")
        r_used, k_step, k_exp = sem("router_step"), sem("topk_step"), sem("router_exp")
        x_upd = sem("x_updated")
        s_store = sem("stored")
        m_g, m_u, m_t, m_d, m_x, m_s, m_c = (sem(x) for x in ("e_gate_mm", "e_up_mm", "e_turned", "e_down_mm", "e_gathered", "e_sel_turned", "e_combined"))
        v_gu, v_silu, v_xe, v_st, v_y = (sem(x) for x in ("e_rows_out", "e_silu", "e_chosen", "e_sel_t", "e_y"))
        d_selg, d_sel, d_cur, d_prod, d_hi, d_lo, d_add = (sem(x) for x in ("e_selg", "e_sel", "e_cur", "e_prod", "e_hid_hi", "e_hid_lo", "e_added"))
        g_small, s_ws, s_bs, s_gb = sem("gmlp_step"), sem("w_spatial_loaded"), [sem("b_spatial0"), sem("b_spatial1")], sem("gate_b_bias")
        c_step, c_exp = sem("merge_step"), sem("merge_exp")

        used_by, halves = {}, [0]

        def tm_used(ws, key):
            halves[0] += 1
            used_by[ws[0]] = (half_used, halves[0])
            used_by[ws[1]] = (filled, fill_no(key))

        for i, w in enumerate(W_IN):
            used_by[w] = (filled, fill_no(("in", 2 * i + 1)))
        tm_used(W_V[0], ("v", 3))
        for h in range(2):
            tm_used(W_OUT[h], ("wout", h, 3))
        used_by[W_PROJ] = (filled, fill_no(("proj", 1, 3)))
        for i in range(NE * SLABS_E):
            used_by[WE0 + i] = (e_used, i + 4)
        for h in range(2):
            tm_used(W_PGATE[h], ("pgate", h, 3))
        for h in range(4):
            tm_used(W_AV[h], ("av", h, 3))
        for g in range(8):
            used_by[W_AU[g]] = (filled, fill_no(("au", g, 1)))
            used_by[W_AZ[g]] = (filled, fill_no(("az", g, 1)))
            if g % 4 == 3:
                for h in range(2):
                    tm_used(W_AO[g // 4][h], ("ao", g // 4, h, 3))
        for g in range(NG):
            used_by[W_K[g]] = (filled, fill_no(("k2", 2 * g + 1)))
            used_by[W_VK[g]] = (filled, fill_no(("v2", g, 3)))
        for g in range(NG):
            for i in range(4):
                used_by[W_Q[g][i]] = (filled, fill_no(("q2", g, 2 * i + 1)))
        for i in range(4):
            used_by[W_Z[i]] = (filled, fill_no(("z", 2 * i + 1)))
        for h in range(2):
            tm_used(W_BO[h], ("bo", h, 3))

        def slot(n):
            return n % RING

        def raw3(n, k):
            return RAW[slot(n)][:, :].rearrange("p (k n) -> p k n", k=k)

        def tile_of(ap, g, t):
            if g == 0:
                return ap[:, t * P:(t + 1) * P]
            return ap.rearrange("p (i r) -> p r i", r=NT)[:, t, :]

        def to_order(ap, g):
            return ap if g == 0 else ap.rearrange("p (i r) -> p r i", r=NT)

        def in_order(ap, g):
            return ap if g == 0 else ap.rearrange("p (r i) -> p r i", r=NT)

        KEYS1 = {0: (0, 1), 1: (0, 1, 2), 2: (1, 2, 3), 3: (2, 3)}
        WINC = {0: 384, 1: 0, 2: 0, 3: 640}
        BJ = {0: 16, 1: 0, 2: 0, 3: 0}

        def item1(j):
            tr, h = ITEMS1[j]
            t = NT - 1 - tr
            kts = KEYS1[t]
            return tr, t, h, kts, len(kts) * P

        def item2(g, j):
            t, h = j // H2, j % H2
            kts = (t - 1, t) if g == 0 and t > 0 else (t,)
            return t, h, kts, len(kts) * P

        slopes = [2.0 ** (-8.0 * (i + 1) / (NG * H2)) for i in range(NG * H2)]


        LGX = at("logits_x", 193.5, [P, NT, NE])
        FSM = at("ffn_small2", 194, [P, 64])
        RMX, RSM, RRC = FSM[:, 0:4], FSM[:, 4:8], FSM[:, 8:12]
        POSC, POSN, AFFC = FSM[:, 12:16], FSM[:, 16:20], FSM[:, 20:24]
        M8 = FSM[0:NE, 32:40]
        ONEROW = bass.AP(ONES.ap().tensor, ONES.ap().offset, [[ONES.ap().ap[0][0], NE], [0, S]])
        V_NORMED, MERGED = 7, 14
        e_sq, v_sq, g_act, x_mul, s_ada, zeroed, g_mul, v_xg, m_xt = sem("e_sq"), sem("v_sq"), sem("gmlp_act"), sem("x_mul"), sem("ada_scaled"), sem("zeroed"), sem("gated_values"), sem("e_chosen_rows"), sem("e_chosen_turned")

        def k2_final(dve, head_final, j):
            g = j // 2
            head_final(("k2", j), ("k2ss", j), 8 + j, pcol("k_norm_g_2"), in_order(K2[:, g, j % 2, :], g),
                       lambda x: to_order(x, g))

        def q2_final(dve, head_final, g, j):
            head_final(("q2", g, j), ("q2ss", g, j), 14 + 8 * g + j, QG2, in_order(Q2[:, j, :], g),
                       lambda x: to_order(x, g))

        block = ctx.enter_context(nc.Block())

        @block.sync
        def _(sp):
            sp.dma_start(CE[:, :], c_early).then_inc(s_const, 16)
            for name, rows in COL_ROWS:
                src = a[name]
                flat = src if len(src.shape) == 1 else src[0]
                for j in range(2 if name in ("q_norm", "k_norm") else 1):
                    n = min(flat.shape[0], rows * P)
                    sp.dma_start(ROWS_IN[COL[name]:COL[name] + rows, j * HD1:j * HD1 + n // rows],
                                 flat[0:n].rearrange("(r c) -> r c", r=rows)).then_inc(s_rows, 16)

            def load(n):
                src, _, _ = stream[n]
                if n >= RING:
                    _, kind, i = stream[n - RING]
                    if kind == "W":
                        sp.wait_ge(lo_ready, i + 1)
                    else:
                        sp.wait_ge(ada_step, ada_done(i))
                sp.dma_start(raw3(n, src.shape[1]), src).then_inc(loaded[slot(n)], 16)

            for n in range(N_E - 1):
                load(n)
                if n == 1:
                    sp.dma_start(CW[:, :], c_wins).then_inc(s_wins, 16)
                    sp.dma_start(GATE_A[:, :], bc(a["a_ada_b_2"], 2 * D, D)).then_inc(s_ga, 16)
            sp.wait_ge(filled, fill_no(("pool", 3)))
            sp.dma_start(GROW[:, :], bc(a["norm_ffn"], 0, D)).then_inc(s_grow, 16)
            sp.dma_start(CL[:, :], c_late).then_inc(s_late, 16)
            sp.dma_start(WR[:, :, :], a["w_router"][0].rearrange("(k p) e -> p k e", p=P)).then_inc(s_wr, 16)
            sp.dma_start(PTOK[:, :, :], a["p"][0, 0].rearrange("(t p) d -> p t d", p=P)).then_inc(s_p, 16)
            load(N_E - 1)

            wg, wu = (a[x][0].rearrange("e (k p) f -> e p k f", p=P) for x in ("w_gate", "w_up"))
            wd = a["w_down"][0].rearrange("e (k p) d -> e p k d", p=P)
            with sp.Fori(0, NE) as e:
                for i in range(SLABS_E):
                    sp.wait_ge(lo_ready, e * SLABS_E + (WE0 + i - RING + 1))
                    if i < 16:
                        w, h, k = (wg, wu)[i // 4 % 2], i // 8, 2 * (i % 4)
                        src = w[e, :, k:k + 2, h * D:(h + 1) * D]
                    else:
                        k = 2 * (i - 16)
                        src = wd[e, :, k:k + 2, :]
                    sp.dma_start(raw3(N_E + i, 2), src).then_inc(loaded[slot(N_E + i)], 16)
            sp.wait_ge(n_xn, 8)
            sp.dma_start(GROW[:, :], bc(a["norm_ple_post"], 0, D)).then_inc(s_grow, 16)
            n_after = N_E + NE * SLABS_E
            for n in range(n_after, len(stream)):
                _, kind, i = stream[n]
                if kind == "W" and i == W_AV[0][0]:
                    sp.wait_ge(d_add, 8 * NE + 8)
                    sp.dma_start(WS_IN[:, :, :], a["a_w_spatial_2"][0].rearrange("g t s -> t g s")).then_inc(s_ws, 16)
                    sp.dma_start(GATE_B[:, :], bc(a["b_ada_b_2"], 2 * D, D)).then_inc(s_gb, 16)
                if kind == "W" and i in W_AU:
                    g = W_AU.index(i)
                    if g >= 2:
                        sp.wait_ge(freed["dve"], fills[("am", g - 2, 1)][2])
                    sp.dma_start(BS[g % 2][:, :], bc(a["a_b_spatial_2"], g * P, P)).then_inc(s_bs[g % 2], 16)
                load(n)
            sp.wait_ge(x_upd, 32)
            sp.dma_start(out[0].rearrange("(t p) d -> p t d", p=P), X[:, :, :]).then_inc(s_store, 16)
            sp.wait_ge(s_store, 16)

        @block.gpsimd
        def _(pool):
            nc.gpsimd.memset(RPB[:, :, :], 0.0).then_inc(s_pad, 1)
            pool.wait_ge(s_pad, 1)
            pool.dma_start(RPB[:, :, WIN:WIN + 31], a["rpb"][0]).then_inc(s_rpb, 16)
            pool.wait_ge(s_rpb, 16)
            for r in range(ROWS):
                pool.dma_start(rpb_wide[r].rearrange("(h k) j -> h (k j)", h=H1),
                               RPB[:, r:r + ROWS, :].rearrange("h k j -> h (k j)")).then_inc(s_rpb, 16)
            pool.wait_ge(s_rpb, 16 * (ROWS + 1))
            def ada_block(b, acc):
                for i in range(4 * b, 4 * b + 4):
                    n = n_of["A"][i]
                    prod = raw3(n, 2)
                    done = ada_done(i - 1)
                    pool.wait_ge(loaded[slot(n)], 16 * (n // RING + 1))
                    nc.gpsimd.tensor_tensor(prod, prod, spread(CSIL[:, 2 * (i % 4):2 * (i % 4) + 2], D),
                                            ALU.mult).then_inc(ada_step, 1)
                    pool.wait_ge(ada_step, done + 1)
                    if i % 4 == 0:
                        if b > 0:
                            key = ("ada", b - 1) if ("ada", b - 1) in fills else ("ada", b - 1, 1)
                            pool.wait_ge(filled, fill_no(key))
                        nc.gpsimd.tensor_tensor(acc[:, :], prod[:, 0, :], prod[:, 1, :], ALU.add).then_inc(ada_step, 1)
                    else:
                        nc.gpsimd.tensor_tensor(acc[:, :], acc[:, :], prod[:, 0, :], ALU.add).then_inc(ada_step, 1)
                        pool.wait_ge(ada_step, done + 2)
                        nc.gpsimd.tensor_tensor(acc[:, :], acc[:, :], prod[:, 1, :], ALU.add).then_inc(ada_step, 1)

            pool.wait_ge(s_csil, 1)
            ada_block(0, ACC1)
            for c in range(16):
                pool.dma_start(BIAS[c * ROWS:(c + 1) * ROWS, :, :],
                               bass.AP(rpb_wide.tensor, c, [[H1 * ROWS * 63, ROWS], [63, H1 * ROWS], [1, 48]])
                               ).then_inc(s_bias, 16)
            ada_block(1, ACC1)
            ada_block(2, ACC1)
            pool.wait_ge(filled, fill_no(("v", 3)))
            pool.dma_start(WP[:, :, :], a["w_pool"][0].rearrange("g c d -> c g d")).then_inc(s_wp, 16)
            pool.wait_ge(freed["act"], fills[("in", 3)][2])
            n, wins_ = 0, (W2, W4, W8, W16)
            for g in range(4):
                if g:
                    pool.wait_ge(p_step, n)
                pool.dma_start(CNT[:, :], bc(c_cnt, g * S, S)).then_inc(s_cnt, 16)
                cur = UP[:, g, :]
                lo, hi, reach = 0, S + 16, 1
                for k in range(g + 1):
                    nxt = wins_[k][:, :]
                    if n:
                        pool.wait_ge(p_step, n)
                    if k == 0:
                        lo += 1
                        nc.gpsimd.tensor_tensor(nxt[:, lo:hi], cur[:, lo - 1:hi - 1], cur[:, lo:hi],
                                                ALU.add).then_inc(p_step, 1)
                    else:
                        lo, hi = lo + reach, hi - reach
                        nc.gpsimd.tensor_tensor(nxt[:, lo:hi], cur[:, lo - reach:hi - reach],
                                                cur[:, lo + reach:hi + reach], ALU.add).then_inc(p_step, 1)
                        reach *= 2
                    n += 1
                    cur = nxt
                pool.wait_ge(p_step, n)
                pool.wait_ge(s_cnt, 16 * (g + 1))
                nc.gpsimd.tensor_tensor(DT[:, g, :], cur[:, 8:8 + S], CNT[:, :], ALU.mult).then_inc(p_step, 1)
                n += 1
                pool.wait_ge(p_step, n)
                nc.gpsimd.tensor_tensor(DT[:, g, :], DT[:, g, :], UP[:, g, 8:8 + S],
                                        ALU.subtract).then_inc(p_step, 1)
                n += 1
            pool.wait_ge(d_add, 8 * NE + 8)
            for b in range(3, 8):
                ada_block(b, ACC2)

        POOL_STEPS = 1 + 2 + 3 + 4 + 2 * 4

        @block.tensor
        def _(pe):
            mm = nc.tensor.matmul
            at_fill = [0]

            def begin(key):
                assert order[at_fill[0]] == key, (order[at_fill[0]], key)
                at_fill[0] += 1
                i, _, _, r0 = fills[key]
                if i - r0 >= 8:
                    _, eng, n, _ = fills[order[i - 8]]
                    pe.wait_ge(freed[eng], n)
                return bank(key)

            def norm(k):
                banks = []
                for chunks in (range(0, 6), range(6, KD)):
                    if k == 2 and chunks[0] == 6:
                        pe.wait_ge(d_add, 8 * NE + 8)
                    for t in range(NT):
                        pe.wait_ge(n_xn, 4 * min(k, 4) + t + 1)
                        for kc in chunks:
                            if t == 0:
                                banks.append(begin(("norm", k, kc)))
                            last = nc.tensor.transpose(banks[kc][:, t * P:(t + 1) * P],
                                                       XNORM[k][:, t, kc * P:(kc + 1) * P], ident)
                            if t == NT - 1:
                                last.then_inc(filled, 1)

            def slab_ready(w):
                pe.wait_ge(lo_ready, w + 1)
                return WHI[w % 2], WLO[w % 2]

            def fm_chunk(w, c, key, ah, al, f0=None):
                hi, lo = slab_ready(w)
                b = begin(key)
                for kc in range(KD):
                    if f0 is not None:
                        pe.wait_ge(f_lo, f0 + kc + 1)
                    cols = slice(kc * 256 + c * P, kc * 256 + (c + 1) * P)
                    mm(b[:, :], hi[:, cols], ah[:, kc, :], start=(kc == 0), stop=False)
                    mm(b[:, :], hi[:, cols], al[:, kc, :], start=False, stop=False)
                    last = mm(b[:, :], lo[:, cols], ah[:, kc, :], start=False, stop=(kc == KD - 1))
                last.then_inc(filled, 1)

            def tm_unit(ws, keys, ah, al, f0=None):
                banks = []
                for s in range(2):
                    hi, lo = slab_ready(ws[s])
                    for t in range(NT):
                        if s == 0:
                            banks.append(begin(keys[t]))
                        b = banks[t]
                        for k in range(4):
                            kc = 4 * s + k
                            if f0 is not None and t == 0:
                                pe.wait_ge(f_lo, f0 + kc + 1)
                            a_hi, a_lo = ah[:, kc, t * P:(t + 1) * P], al[:, kc, t * P:(t + 1) * P]
                            r = slice(k * 512, (k + 1) * 512)
                            mm(b[:, :], a_hi, hi[:, r], start=(kc == 0), stop=False)
                            mm(b[:, :], a_hi, lo[:, r], start=False, stop=False)
                            last = mm(b[:, :], a_lo, hi[:, r], start=False, stop=(kc == KD - 1))
                        if s == 1:
                            last.then_inc(filled, 1)
                    if s == 0:
                        last.then_inc(half_used, 1)

            def head_squares(key, j, ones_ap):
                pe.wait_ge(h_sq, j + 1)
                b = begin(key)
                mm(b[:, :], ones_ap, SQ[j % 2][:, :], start=True, stop=True).then_inc(filled, 1)

            def ada_cols(b_, acc):
                pe.wait_ge(ada_step, ada_done(4 * b_ + 3))
                b = begin(("ada", b_))
                for c in range(KD):
                    last = mm(b[:, c:c + 1], acc[:, c * P:(c + 1) * P], ONES[:, 0:1], start=True, stop=True)
                last.then_inc(filled, 1)

            def ada_rows(b_, acc):
                pe.wait_ge(ada_step, ada_done(4 * b_ + 3))
                for h in range(2):
                    b = begin(("ada", b_, h))
                    mm(b[:, :], ONES[:, :], acc[:, h * 512:(h + 1) * 512], start=True, stop=True).then_inc(filled, 1)

            pe.wait_ge(s_const, 16)
            pe.wait_ge(s_rows, 16 * (len(COL_ROWS) + 2))
            b = begin(("cols",))
            nc.tensor.transpose(b[:, 0:NCOL], ROWS_IN[0:NCOL, :], ident[0:NCOL, 0:NCOL]).then_inc(filled, 1)
            pe.wait_ge(s_init, 4)
            norm(0)
            for j in range(12):
                fm_chunk(W_IN[j // 2], j % 2, ("in", j), AH, AL, 0 if j == 0 else None)
                if j >= 5:
                    head_squares(("inss", j - 1), j - 5, blocks64)
                if j == 9:
                    ada_cols(0, ACC1)
            head_squares(("inss", 11), 7, blocks64)
            tm_unit(W_V[0], [("v", t) for t in range(NT)], AH, AL)

            pe.wait_ge(s_wins, 16)
            pe.wait_ge(freed["dve"], fills[("in", 11)][2])
            pe.wait_ge(freed["act"], fills[("v", 3)][2])
            n_items = len(ITEMS1)
            for j in range(n_items + 3):
                if j < n_items:
                    tr, t, h, kts, n = item1(j)
                    rows = slice((h % 2) * HD1, (h % 2 + 1) * HD1)
                    b = begin(("a1s", j))
                    mm(b[:, 0:n], ident_bf, CW[:, WINC[t]:WINC[t] + n], start=True, stop=False)
                    mm(b[:, 0:n], Q1[rows, h // 2, tr * P:(tr + 1) * P],
                       K1[rows, h // 2, kts[0] * P:kts[0] * P + n], start=False, stop=True).then_inc(filled, 1)
                if 2 <= j < n_items + 2:
                    _, _, _, kts, n = item1(j - 2)
                    pe.wait_ge(a_exp, j - 1)
                    b = begin(("a1t", j - 2))
                    for i in range(len(kts)):
                        last = nc.tensor.transpose(b[:, i * P:(i + 1) * P], P1[j % 2][:, i * P:(i + 1) * P], ident)
                    last.then_inc(filled, 1)
                if j >= 3:
                    _, _, h, kts, n = item1(j - 3)
                    pe.wait_ge(freed["act"], fills[("a1t", j - 3)][2])
                    b = begin(("a1o", j - 3))
                    for i, kt in enumerate(kts):
                        last = mm(b[:, 0:HD1], PT1[(j - 3) % 2][:, i * P:(i + 1) * P], V1[:, kt, h * HD1:(h + 1) * HD1],
                                  start=(i == 0), stop=(i == len(kts) - 1))
                    last.then_inc(filled, 1)
                if j == 12:
                    ada_cols(1, ACC1)
            ada_rows(2, ACC1)
            pe.wait_ge(s_wp, 16)
            pe.wait_ge(p_step, POOL_STEPS)
            for g in range(4):
                b = begin(("pool", g))
                mm(b[:, :], WP[:, g, :], DT[:, g, :], start=True, stop=True).then_inc(filled, 1)
            pe.wait_ge(freed["dve"], fills[("a1o", n_items - 1)][2])
            for c in range(4):
                b = begin(("ot1", c))
                for t in range(NT):
                    last = nc.tensor.transpose(b[:, t * P:(t + 1) * P], O1[:, t, c * P:(c + 1) * P], ident)
                last.then_inc(filled, 1)
            for h in range(2):
                tm_unit(W_OUT[h], [("wout", h, t) for t in range(NT)], BH, BL, 8 if h == 0 else None)

            pe.wait_ge(s_wr, 16)
            norm(1)
            lg = begin(("logits",))
            for kc in range(KD):
                pe.wait_ge(freed["act"], fills[("norm", 1, kc)][2])
                for t in range(NT):
                    last = mm(lg[:, t * NE:(t + 1) * NE], FULL[kc % 2][:, t * P:(t + 1) * P], WR[:, kc, :],
                              start=(kc == 0 and t == 0), stop=(kc == KD - 1), skip_group_check=True)
                    if kc == 0 and t == 0:
                        last.then_inc(filled, 1)
                last.then_inc(r_used, 1)
            pe.wait_ge(k_step, 5)
            b = begin(("aff_t",))
            for t in range(NT):
                last = nc.tensor.transpose(b[0:NE, t * P:(t + 1) * P], AFF[:, t, 0:NE], ident)
            last.then_inc(filled, 1)
            pe.wait_ge(s_p, 16)
            for c in range(2):
                b = begin(("pt", c))
                for t in range(NT):
                    last = nc.tensor.transpose(b[:, t * P:(t + 1) * P], PTOK[:, t, c * P:(c + 1) * P], ident)
                last.then_inc(filled, 1)
            pe.wait_ge(f_lo, 18)
            hi, lo = slab_ready(W_PROJ)
            for h in range(2):
                for t in range(NT):
                    b = begin(("proj", h, t))
                    for k in range(2):
                        r = slice(k * D + h * 512, k * D + (h + 1) * 512)
                        p_h, p_l = PH[:, k, t * P:(t + 1) * P], PL[:, k, t * P:(t + 1) * P]
                        mm(b[:, :], p_h, hi[:, r], start=(k == 0), stop=False)
                        mm(b[:, :], p_h, lo[:, r], start=False, stop=False)
                        last = mm(b[:, :], p_l, hi[:, r], start=False, stop=(k == 1))
                    last.then_inc(filled, 1)
            pe.wait_ge(k_step, 5 + 16 + 3)
            b = begin(("pos_t",))
            for t in range(NT):
                last = nc.tensor.transpose(b[:, t * NE:(t + 1) * NE], RANK[:, t * P:(t + 1) * P], ident[0:NE, 0:NE])
            last.then_inc(filled, 1)

            def gather(h):
                for part, src in enumerate((TH, TL)):
                    for t in range(NT):
                        o = CAP * (1 - part)
                        last = mm(PS[6 + h][:, :], SEL[:, t, o:o + P], src[:, t, h * 512:(h + 1) * 512],
                                  start=(part == 0 and t == 0), stop=(part == 1 and t == NT - 1))
                if h == 1:
                    last.then_inc(m_x, 1)

            def turn_chosen(n):
                pe.wait_ge(v_xg, n)
                for c in range(KD):
                    last = nc.tensor.transpose(PS[7 - c // 4][:, (c % 4) * P:(c % 4 + 1) * P],
                                               XG[:, c * P:(c + 1) * P], ident)
                last.then_inc(m_xt, 1)

            def turn_selection():
                for t in range(NT):
                    last = mm(PS[6][:, t * P:(t + 1) * P], SELG[:, t, :], ident, start=True, stop=True)
                last.then_inc(m_s, 1)

            def turn(src, b):
                for c in range(8):
                    last = mm(b[:, c * CAP:(c + 1) * CAP], src[:, c * P:(c + 1) * P], stack64, start=True, stop=True)
                return last

            def expert_slab(i, lhs, banks, first, final):
                hi, lo = WHI_E[i % 3], WLO_E[i % 3]
                for k in range(2):
                    for n in range(2):
                        r = slice(k * D + n * 512, k * D + (n + 1) * 512)
                        mm(banks[n][:, :], lhs[k], hi[:, r], start=(first and k == 0), stop=False)
                        last = mm(banks[n][:, :], lhs[k], lo[:, r], start=False, stop=(final and k == 1))
                last.then_inc(e_used, 1)

            def combine(j, base_):
                t, h = j // 2, j % 2
                if j >= 2:
                    pe.wait_ge(d_add, base_ + (j - 1))
                mm(PS[6 + j % 2][:, :], SELT[:, t * P:(t + 1) * P], Y[:, h * 512:(h + 1) * 512],
                   start=True, stop=True).then_inc(m_c, 1)

            pe.sem_inc(e_used, 3)
            pe.wait_ge(freed["act"], COUNT_BEFORE_E["act"])
            pe.wait_ge(freed["dve"], COUNT_BEFORE_E["dve"])
            pe.wait_ge(t_lo, 4)
            pe.wait_ge(zeroed, 4)
            pe.wait_ge(d_sel, 1)
            gather(0)
            gather(1)
            turn_chosen(1)
            with pe.Fori(0, NE) as e:
                pe.wait_ge(v_xe, e + 1)
                pe.wait_ge(d_selg, e + 1)
                turn_selection()
                for i in range(16):
                    if i in (0, 4, 8, 12):
                        pe.wait_ge(v_gu, e * 4 + (3 + i // 4))
                    if i == 12:
                        pe.wait_ge(d_add, e * 8 + 8)
                        turn(GS, PS[6])
                        turn(US, PS[7]).then_inc(m_t, 1)
                    pe.wait_ge(lo_ready, e * SLABS_E + (WE0 + i + 1))
                    q = i % 4
                    two = (PS[0], PS[1]) if i // 4 % 2 == 0 else (PS[2], PS[3])
                    expert_slab(i, [XE[:, 2 * q + k, :] for k in range(2)], two, q == 0, q == 3)
                    if i == 1:
                        pe.wait_ge(v_y, e + 1)
                        pe.wait_ge(v_st, e + 1)
                    if 1 <= i < 9:
                        combine(i - 1, e * 8)
                pe.wait_ge(d_lo, e * 2 + 1)
                for q in range(8):
                    if q == 2:
                        pe.wait_ge(v_gu, e * 4 + 8)
                        pe.wait_ge(d_prod, e * 2 + 1)
                        turn(GS, PS[6])
                        turn(US, PS[7]).then_inc(m_t, 1)
                    if q == 4:
                        pe.wait_ge(d_lo, e * 2 + 2)
                        pe.wait_ge(d_sel, e + 2)
                    if q in (4, 5):
                        gather(q - 4)
                    if q == 7:
                        turn_chosen(e + 2)
                    pe.wait_ge(lo_ready, e * SLABS_E + (WE0 + 16 + q + 1))
                    expert_slab(16 + q, [HM[:, 2 * q + k, :] for k in range(2)], (PS[4], PS[5]), q == 0, q == 7)
            pe.wait_ge(d_selg, NE + 1)
            turn_selection()
            pe.wait_ge(v_y, NE + 1)
            pe.wait_ge(v_st, NE + 1)
            for j in range(8):
                combine(j, 8 * NE)

            norm(2)
            for h in range(2):
                tm_unit(W_PGATE[h], [("pgate", h, t) for t in range(NT)], AH, AL, 18 if h == 0 else None)

            norm(3)
            pe.wait_ge(s_ws, 16)
            for i in range(2):
                b = begin(("ws", i))
                for g in range(4):
                    last = nc.tensor.transpose(b[:, g * P:(g + 1) * P], WS_IN[:, 4 * i + g, :], ident)
                last.then_inc(filled, 1)
            for h in range(4):
                tm_unit(W_AV[h], [("av", h, t) for t in range(NT)], AH, AL, 26 if h == 0 else None)
                if h == 2:
                    ada_cols(3, ACC2)
            for g in range(8):
                for c in range(2):
                    fm_chunk(W_AU[g], c, ("au", g, c), AH, AL)
                for c in range(2):
                    fm_chunk(W_AZ[g], c, ("az", g, c), AH, AL)
                if g == 0:
                    pe.wait_ge(g_small, V_NORMED)
                for c in range(2):
                    b = begin(("am", g, c))
                    e0 = g * 256 + c * P
                    for t in range(NT):
                        last = mm(b[:, t * P:(t + 1) * P], VV[:, t, e0:e0 + P], WST[:, g, :], start=True, stop=True)
                    last.then_inc(filled, 1)
                if g in (0, 2, 4):
                    ada_cols(4 + g // 2, ACC2)
                if g == 7:
                    ada_rows(7, ACC2)
                if g % 4 == 3:
                    for h in range(2):
                        tm_unit(W_AO[g // 4][h], [("ao", g // 4, h, t) for t in range(NT)], BH, BL,
                                34 + 8 * (g // 4) if h == 0 else None)

            norm(4)
            for j in range(6):
                fm_chunk(W_K[j // 2], j % 2, ("k2", j), AH, AL, 50 if j == 0 else None)
                if j >= 1:
                    head_squares(("k2ss", j - 1), 8 + j - 1, ONES[:, :])
            head_squares(("k2ss", 5), 8 + 5, ONES[:, :])
            for g in range(NG):
                hi, lo = slab_ready(W_VK[g])
                for t in range(NT):
                    b = begin(("v2", g, t))
                    for kc in range(KD):
                        a_hi, a_lo = tile_of(AH[:, kc, :], g, t), tile_of(AL[:, kc, :], g, t)
                        r = slice(kc * 256, (kc + 1) * 256)
                        mm(b[:, 0:256], a_hi, hi[:, r], start=(kc == 0), stop=False)
                        mm(b[:, 0:256], a_hi, lo[:, r], start=False, stop=False)
                        last = mm(b[:, 0:256], a_lo, hi[:, r], start=False, stop=(kc == KD - 1))
                    last.then_inc(filled, 1)
            norm(5)
            for g in range(NG):
                for j in range(H2):
                    fm_chunk(W_Q[g][j // 2], j % 2, ("q2", g, j), AH, AL, 58 if g + j == 0 else None)
                    if j >= 1:
                        head_squares(("q2ss", g, j - 1), 14 + 8 * g + j - 1, ONES[:, :])
                head_squares(("q2ss", g, 7), 14 + 8 * g + 7, ONES[:, :])
                pe.wait_ge(freed["dve"], fills[("q2", g, 7)][2])
                pe.wait_ge(freed["act"], fills[("v2", NG - 1, 3)][2])
                n_items, j0 = NT * H2, 32 * (g + 1)
                tag = f"b{g}"
                for j in range(n_items + 3):
                    if j < n_items:
                        t, h, kts, n = item2(g, j)
                        b = begin((tag + "s", j))
                        mm(b[:, 0:n], Q2[:, h, t * P:(t + 1) * P], K2[:, g, h // 4, kts[0] * P:kts[0] * P + n],
                           start=True, stop=True).then_inc(filled, 1)
                    if 2 <= j < n_items + 2:
                        _, _, kts, n = item2(g, j - 2)
                        pe.wait_ge(a_exp, j0 + j - 1)
                        b = begin((tag + "t", j - 2))
                        for i in range(len(kts)):
                            last = nc.tensor.transpose(b[:, i * P:(i + 1) * P], P2[j % 2][:, i * P:(i + 1) * P], ident)
                        last.then_inc(filled, 1)
                    if j >= 3:
                        _, h, kts, n = item2(g, j - 3)
                        pe.wait_ge(freed["act"], fills[(tag + "t", j - 3)][2])
                        b = begin((tag + "o", j - 3))
                        for i, kt in enumerate(kts):
                            last = mm(b[:, 0:P], PT2[(j - 3) % 2][:, i * P:(i + 1) * P],
                                      V2[:, g, kt, (h // 4) * P:(h // 4 + 1) * P],
                                      start=(i == 0), stop=(i == len(kts) - 1))
                        last.then_inc(filled, 1)

            for g in range(NG):
                for key, src in ((("nm_t", g), NM2), (("l_t", g), L2)):
                    b = begin(key)
                    for t in range(NT):
                        last = nc.tensor.transpose(b[0:H2, t * P:(t + 1) * P], src[:, g, t * H2:(t + 1) * H2], ident)
                    last.then_inc(filled, 1)
            for h in range(2):
                fm_chunk(W_Z[0], h, ("z", h), AH, AL)
            pe.wait_ge(c_step, MERGED)
            for g in range(NG):
                b = begin(("wg", g))
                for t in range(NT):
                    last = nc.tensor.transpose(b[:, t * H2:(t + 1) * H2], LT2[g][:, t * P:(t + 1) * P], ident[0:H2, 0:H2])
                last.then_inc(filled, 1)
            for h in range(H2):
                pe.wait_ge(c_step, MERGED + 12 * (h + 1))
                b = begin(("comb", h))
                for g in range(NG):
                    for t in range(NT):
                        last = mm(tile_of(b[:, :], g, t), O2[g][:, h, t, :], DG[h % 2][:, g * NT + t, :],
                                  start=(g == 0 and t == 0), stop=(g == NG - 1), skip_group_check=True)
                last.then_inc(filled, 1)
                if h + 2 < H2:
                    fm_chunk(W_Z[h // 2 + 1], h % 2, ("z", h + 2), AH, AL)
            for h in range(2):
                tm_unit(W_BO[h], [("bo", h, t) for t in range(NT)], BH, BL, 66 if h == 0 else None)

        JUNK = at("junk", 148, [P, D])

        @block.scalar
        def _(act):
            for t in range(NT):
                act.dma_start(X[:, t, :], a["x"][0, t * P:(t + 1) * P, :]).then_inc(s_x, 16)
            split_at, f = [0], [0]

            def split_upto(w_last):
                while split_at[0] <= w_last:
                    w = split_at[0]
                    n = n_of["W"][w]
                    act.wait_ge(loaded[slot(n)], 16 * (n // RING + 1))
                    if w >= 2:
                        act.wait_ge(*used_by[w - 2])
                    nc.scalar.copy(WHI[w % 2][:, :], RAW[slot(n)][:, :]).then_inc(hi_ready, 1)
                    split_at[0] += 1

            def take(key):
                act.wait_ge(filled, fill_no(key))
                return bank(key)

            def stats(k, x_ready):
                for t in range(NT):
                    act.wait_ge(*x_ready(t))
                    nc.scalar.activation(XNORM[k][:, t, :], X[:, t, :], ACT.Square, accum_out=SS[:, t:t + 1]
                                         ).then_inc(n_sq, 1)
                    act.wait_ge(n_ms, 4 * k + t + 1)
                    nc.scalar.activation(STD[:, t:t + 1], MS[:, t:t + 1], ACT.Sqrt).then_inc(n_sqrt, 1)

            def full(key, out_ap=None, in_ap=None, mul=1.0, add=0.0):
                b = take(key)
                if f[0] >= 2:
                    act.wait_ge(f_lo, f[0] - 1)
                dst = FULL[f[0] % 2][:, :]
                nc.scalar.activation(dst if out_ap is None else out_ap(dst), b[:, :] if in_ap is None else in_ap(b[:, :]),
                                     ACT.Identity, bias=add, scale=mul).then_inc(freed["act"], 1)
                f[0] += 1

            def norm_full(k):
                for kc in range(KD):
                    full(("norm", k, kc), mul=NORM_MUL[k](kc), add=NORM_ADD[k](kc) if k in NORM_ADD else 0.0)

            def head_square(key, j):
                nc.scalar.activation(SQ[j % 2][:, :], take(key)[:, :], ACT.Square).then_inc(h_sq, 1)

            def head_std(key, j, width, reader=None):
                b = take(key)
                if reader is not None:
                    act.wait_ge(freed["dve"], fills[reader][2])
                nc.scalar.activation(FULL[j % 2][:, :], b[:, :], ACT.Sqrt, bias=EPSC, scale=1.0 / width
                                     ).then_inc(freed["act"], 1)

            def attention(tag, n_items, j0, s_buf, p_buf, pt_buf, width, nm, rs):
                for j in range(n_items + 2):
                    if j >= 2:
                        n = width(j - 2)
                        b = take((tag + "t", j - 2))
                        if j >= 4:
                            act.wait_ge(filled, fill_no((tag + "o", j - 4)))
                        nc.scalar.copy(pt_buf[j % 2][:, 0:n], b[:, 0:n]).then_inc(freed["act"], 1)
                    if j < n_items:
                        n = width(j)
                        act.wait_ge(a_nm, j0 + j + 1)
                        if j >= 2:
                            act.wait_ge(filled, fill_no((tag + "t", j - 2)))
                            if tag == "a1":
                                act.wait_ge(a_rr, j - 1)
                        nc.scalar.activation(p_buf[j % 2][:, 0:n], s_buf[j % 2][:, 0:n], ACT.Exp, bias=nm(j),
                                             accum_out=rs(j)).then_inc(a_exp, 1)

            stats(0, lambda t: (s_x, 64))
            act.wait_ge(s_init, 4)
            split_upto(0)
            act.wait_ge(freed["dve"], 1)
            nc.scalar.activation(CSIL, pcol("c_2", 0, KD), ACT.Silu).then_inc(s_csil, 1)
            norm_full(0)
            split_upto(1)
            for j in range(12):
                if j % 2 == 0:
                    split_upto(W_IN[j // 2] + 1)
                if j < 4:
                    b = take(("in", j))
                    nc.scalar.copy(UP[:, j, 8:8 + S].rearrange("p (r c) -> p c r", r=ROWS),
                                   b[:, :].rearrange("p (c r) -> p c r", r=ROWS)).then_inc(freed["act"], 1)
                else:
                    head_square(("in", j), j - 4)
                    if j >= 5:
                        head_std(("inss", j - 1), j - 5, HD1, ("in", j - 3) if j >= 7 else None)
            head_std(("inss", 11), 7, HD1, ("in", 9))
            split_upto(W_V[0][1] + 1)
            for t in range(NT):
                nc.scalar.copy(V1[:, t, :], take(("v", t))[:, :]).then_inc(freed["act"], 1)
            split_upto(W_OUT[0][1])
            attention("a1", len(ITEMS1), 0, S1, P1, PT1, lambda j: item1(j)[4], lambda j: NM[j % 2], lambda j: RS[j % 2])
            for g in range(4):
                full(("pool", g), mul=pcol("pool_scale", g))
            for c in range(4):
                full(("ot1", c), out_ap=lambda x: x.rearrange("p (r c) -> p c r", r=ROWS),
                     in_ap=lambda x: x[:, ::-1].rearrange("p (c r) -> p c r", r=ROWS))
            for h in range(2):
                split_upto(W_OUT[h][1] + 1)
            stats(1, lambda t: (freed["dve"], fills[("wout", 1, t)][2]))
            for t in range(NT):
                act.wait_ge(n_xn, 4 + t + 1)
                nc.scalar.copy(TH[:, t, :], XNORM[1][:, t, :]).then_inc(t_hi, 1)
            for kc in range(KD):
                b = take(("norm", 1, kc))
                if kc >= 2:
                    act.wait_ge(r_used, kc - 1)
                nc.scalar.copy(FULL[kc % 2][:, :], b[:, :]).then_inc(freed["act"], 1)
            act.wait_ge(freed["dve"], fills[("logits",)][2])
            nc.scalar.activation(LGX[:, :, :], LGX[:, :, :], ACT.Exp).then_inc(k_exp, 1)
            act.wait_ge(r_used, KD)
            for c in range(2):
                full(("pt", c))
            for h in range(2):
                for t in range(NT):
                    nc.scalar.copy(E_[:, t, h * 512:(h + 1) * 512], take(("proj", h, t))[:, :]).then_inc(freed["act"], 1)
            for t in range(NT):
                act.wait_ge(freed["act"], fills[("proj", 1, t)][2])
                if t:
                    act.wait_ge(e_sq, t)
                nc.scalar.activation(JUNK[:, :], E_[:, t, :], ACT.Square, accum_out=ESS[:, t:t + 1]).then_inc(e_sq, 1)

            act.wait_ge(*used_by[WE0 - 1])
            act.sem_inc(v_gu, 4)
            act.wait_ge(zeroed, 4)

            def rows_out(dst, b0):
                nc.scalar.copy(dst[:, 0:512], PS[b0][:, :])
                return nc.scalar.copy(dst[:, 512:D], PS[b0 + 1][:, :])

            def chosen_out(n):
                act.wait_ge(m_x, n)
                nc.scalar.copy(XG[:, 0:512], PS[6][:, :])
                nc.scalar.copy(XG[:, 512:D], PS[7][:, :]).then_inc(v_xg, 1)

            chosen_out(1)
            with act.Fori(0, NE) as e:
                for i in range(SLABS_E):
                    n = N_E + i
                    act.wait_ge(loaded[slot(n)], e * (16 * SLABS_E // RING) + 16 * (n // RING + 1))
                    act.wait_ge(e_used, e * SLABS_E + (i + 1))
                    nc.scalar.copy(WHI_E[i % 3][:, :], RAW[slot(n)][:, :]).then_inc(hi_ready, 1)
                    if i == 0:
                        act.wait_ge(m_xt, e + 1)
                        for b in range(2):
                            last = nc.scalar.copy(XE[:, 4 * b:4 * b + 4, :], PS[7 - b][:, :].rearrange("p (c j) -> p c j", c=4))
                        last.then_inc(v_xe, 1)
                    if i == 1:
                        act.wait_ge(m_s, e + 1)
                        nc.scalar.copy(SELT[:, :], PS[6][:, :]).then_inc(v_st, 1)
                    if i == 2:
                        rows_out(Y, 4).then_inc(v_y, 1)
                    if i == 6:
                        rows_out(GS, 0).then_inc(v_gu, 1)
                    if i == 10:
                        rows_out(US, 2).then_inc(v_gu, 1)
                    if i == 14:
                        act.wait_ge(m_t, e * 2 + 1)
                        nc.scalar.activation(SQ[0][:, :], PS[6][:, :], ACT.Silu).then_inc(v_silu, 1)
                        rows_out(GS, 0).then_inc(v_gu, 1)
                    if i == 18:
                        rows_out(US, 2).then_inc(v_gu, 1)
                    if i == 20:
                        act.wait_ge(m_t, e * 2 + 2)
                        nc.scalar.activation(SQ[0][:, :], PS[6][:, :], ACT.Silu).then_inc(v_silu, 1)
                    if i == 23:
                        chosen_out(e + 2)
            act.wait_ge(m_s, NE + 1)
            nc.scalar.copy(SELT[:, :], PS[6][:, :]).then_inc(v_st, 1)
            act.wait_ge(*used_by[WE0 + NE * SLABS_E - 1])
            rows_out(Y, 4).then_inc(v_y, 1)
            split_at[0] = WE0 + NE * SLABS_E

            split_upto(W_PGATE[0][1])
            stats(2, lambda t: (d_add, 8 * NE + 2 * t + 2))
            act.wait_ge(k_step, 25)
            nc.scalar.activation(ERSTD, ESS, ACT.Sqrt).then_inc(k_exp, 1)
            norm_full(2)
            for h in range(2):
                split_upto(W_PGATE[h][1] + 1)
                for t in range(NT):
                    i = 4 * h + t
                    b = take(("pgate", h, t))
                    if i >= 2:
                        act.wait_ge(x_upd, i - 1)
                    nc.scalar.activation(SQ[i % 2][:, :], b[:, :], ACT.Sigmoid).then_inc(freed["act"], 1)

            split_upto(W_AV[0][1])
            stats(3, lambda t: (x_upd, 4 + t + 1))
            norm_full(3)
            n = 0
            for h in range(4):
                split_upto(W_AV[h][1] + 1)
                for t in range(NT):
                    part = VV[:, t, h * 512:(h + 1) * 512]
                    nc.scalar.activation(part, take(("av", h, t))[:, :], ACT.Gelu_apprx_tanh).then_inc(freed["act"], 1)
                    act.wait_ge(freed["act"], fills[("av", h, t)][2])
                    if n >= 2:
                        act.wait_ge(v_sq, n - 1)
                    nc.scalar.activation(SQ[n % 2][:, :], part, ACT.Square, accum_out=SSV[:, 4 * t + h:4 * t + h + 1]
                                         ).then_inc(v_sq, 1)
                    n += 1
            act.wait_ge(g_small, 2)
            nc.scalar.activation(STD, MS, ACT.Sqrt).then_inc(v_sq, 1)
            for g in range(8):
                split_upto(W_AU[g] + 1)
                for c in range(2):
                    b = take(("au", g, c))
                    nc.scalar.activation(b[:, :], b[:, :], ACT.Gelu_apprx_tanh).then_inc(g_act, 1)
                split_upto(W_AZ[g] + 1)
                if g == 4:
                    act.wait_ge(x_upd, 16)
                for c in range(2):
                    b = take(("az", g, c))
                    if g:
                        act.wait_ge(g_mul, 2 * g + c - 1)
                    nc.scalar.activation(SQ[c][:, :], b[:, :], ACT.Silu).then_inc(freed["act"], 1)
                if g % 4 == 3:
                    f[0] += 8
                    for h in range(2):
                        split_upto(W_AO[g // 4][h][1] + 1)

            stats(4, lambda t: (x_upd, 20 + t + 1))
            norm_full(4)
            for j in range(6):
                if j % 2 == 0:
                    split_upto(W_K[j // 2] + 1)
                head_square(("k2", j), 8 + j)
                if j >= 1:
                    head_std(("k2ss", j - 1), 7 + j, P, ("k2", j - 3) if j >= 3 else None)
            head_std(("k2ss", 5), 13, P, ("k2", 3))
            for g in range(NG):
                split_upto(W_VK[g] + 1)
                for t in range(NT):
                    nc.scalar.copy(V2[:, g, t, :], take(("v2", g, t))[:, 0:256]).then_inc(freed["act"], 1)
            act.wait_ge(freed["dve"], fills[("k2", 5)][2])
            norm_full(5)
            for g in range(NG):
                for j in range(H2):
                    if j % 2 == 0:
                        split_upto(W_Q[g][j // 2] + 1)
                    head_square(("q2", g, j), 14 + 8 * g + j)
                    if j >= 1:
                        head_std(("q2ss", g, j - 1), 13 + 8 * g + j, P, ("q2", g, j - 3) if j >= 3 else None)
                head_std(("q2ss", g, 7), 21 + 8 * g, P, ("q2", g, 5))
                split_upto(W_Q[g][3] + 2)
                attention(f"b{g}", NT * H2, 32 * (g + 1), S2, P2, PT2, lambda j, g=g: item2(g, j)[3],
                          lambda j, g=g: NM2[:, g, j:j + 1], lambda j, g=g: L2[:, g, j:j + 1])
            for g in range(NG):
                act.wait_ge(c_step, 3 + g)
                nc.scalar.activation(NT2[g][:, :], NT2[g][:, :], ACT.Exp).then_inc(c_exp, 1)
            for h in range(H2):
                if h % 2 == 0:
                    split_upto(W_Z[h // 2] + 1)
                b = take(("z", h))
                if h >= 2:
                    act.wait_ge(freed["dve"], fills[("comb", h - 2)][2])
                nc.scalar.activation(SQ[h % 2][:, :], b[:, :], ACT.Silu).then_inc(freed["act"], 1)
            for h in range(2):
                split_upto(min(W_BO[h][1] + 1, len(n_of["W"]) - 1))

        @block.vector
        def _(dve):
            split_at, f = [0], [0]
            tt, ts, stt = nc.vector.tensor_tensor, nc.vector.tensor_scalar, nc.vector.scalar_tensor_tensor

            def split_upto(w_last):
                while split_at[0] <= w_last:
                    w = split_at[0]
                    dve.wait_ge(hi_ready, w + 1)
                    tt(WLO[w % 2][:, :], RAW[slot(n_of["W"][w])][:, :], WHI[w % 2][:, :].bitcast(F32),
                       ALU.subtract).then_inc(lo_ready, 1)
                    split_at[0] += 1

            def take(key):
                dve.wait_ge(filled, fill_no(key))
                return bank(key)

            def norm_tile(k, t):
                i, one = 4 * k + t + 1, slice(t, t + 1)
                dve.wait_ge(n_sq, i)
                ts(MS[:, one], SS[:, one], 1.0 / D, EPS, ALU.mult, ALU.add).then_inc(n_ms, 1)
                dve.wait_ge(n_sqrt, i)
                nc.vector.reciprocal(RSTD[:, one], STD[:, one]).then_inc(n_rstd, 1)
                dve.wait_ge(n_rstd, i)
                if k == 1:
                    if t == 0:
                        dve.wait_ge(s_grow, 16)
                    stt(out=XNORM[k][:, t, :], in0=X[:, t, :], scalar=RSTD[:, one], in1=GROW[:, :],
                        op0=ALU.mult, op1=ALU.mult).then_inc(n_xn, 1)
                else:
                    ts(XNORM[k][:, t, :], X[:, t, :], RSTD[:, one], None, ALU.mult).then_inc(n_xn, 1)

            def norm_behind(k, t):
                if t:
                    norm_tile(k, t - 1)
                if t == NT - 1:
                    norm_tile(k, t)

            def split_full(hi, lo, sem_, value, view=None):
                src = FULL[f[0] % 2][:, :]
                if view is not None:
                    src = view(src)
                dve.wait_ge(sem_, value)
                nc.vector.tensor_copy(hi, src).then_inc(f_hi, 1)
                dve.wait_ge(f_hi, f[0] + 1)
                tt(lo, src, hi.bitcast(F32), ALU.subtract).then_inc(f_lo, 1)
                f[0] += 1

            def norm_split(k, perm=False):
                for kc in range(KD):
                    hi, lo = AH[:, kc, :], AL[:, kc, :]
                    if perm:
                        hi, lo = (x.rearrange("p (c r) -> p r c", r=ROWS) for x in (hi, lo))
                    split_full(hi, lo, freed["act"], fills[("norm", k, kc)][2],
                               (lambda x: x.rearrange("p (r c) -> p r c", r=ROWS)) if perm else None)

            def head_final(key, sskey, j, gain, out_ap, view=lambda x: x):
                r = FULL[j % 2][:, :]
                dve.wait_ge(freed["act"], fills[sskey][2])
                nc.vector.reciprocal(r, r).then_inc(h_rec, 1)
                dve.wait_ge(h_rec, j + 1)
                stt(out=out_ap, in0=view(bank(key)[:, :]), scalar=gain, in1=view(r), op0=ALU.mult, op1=ALU.mult
                    ).then_inc(freed["dve"], 1)

            ADA = {0: ("a_add", "a_ada_b_2", None), 1: ("a_mul", "a_ada_b_2", "a_norm_g_2"),
                   3: ("kv_add", "kv_ada_b_2", None), 4: ("kv_mul", "kv_ada_b_2", "kv_norm_g_2"),
                   5: ("b_add", "b_ada_b_2", None), 6: ("b_mul", "b_ada_b_2", "b_norm_g_2")}

            def ada_out(b_):
                dst, bias, gain = ADA[b_]
                b = take(("ada", b_))
                if gain is None:
                    tt(ADC[dst], b[:, 0:KD], pcol(bias, 0, KD), ALU.add).then_inc(freed["dve"], 1)
                else:
                    tt(ADT, b[:, 0:KD], pcol(bias, KD, KD), ALU.add).then_inc(freed["dve"], 1)
                    dve.wait_ge(freed["dve"], fills[("ada", b_)][2])
                    stt(out=ADC[dst], in0=ADT, scalar=1.0, in1=pcol(gain, 0, KD), op0=ALU.add, op1=ALU.mult
                        ).then_inc(s_ada, 1)

            def ada_gate(b_, gate, s_bias_):
                dve.wait_ge(s_bias_, 16)
                for h in range(2):
                    b = take(("ada", b_, h))
                    part = gate[:, h * 512:(h + 1) * 512]
                    tt(part, b[:, :], part, ALU.add).then_inc(freed["dve"], 1)

            def gated_out(keys, gate, norm=None):
                for key in keys:
                    h, t = key[-2:]
                    i = x_parts[0]
                    x_parts[0] += 1
                    b = take(key)
                    if i >= 2:
                        dve.wait_ge(x_upd, 8 + i - 1)
                    tt(SQ[i % 2][:, :], b[:, :], gate[:, h * 512:(h + 1) * 512], ALU.mult).then_inc(freed["dve"], 1)
                    dve.wait_ge(freed["dve"], fills[key][2])
                    part = X[:, t, h * 512:(h + 1) * 512]
                    tt(part, part, SQ[i % 2][:, :], ALU.add).then_inc(x_upd, 1)
                    if norm is not None:
                        norm_behind(norm, t)

            x_parts = [0]
            nc.vector.memset(ONES[:, :], 1.0).then_inc(s_init, 1)
            nc.vector.memset(EPSC, EPS).then_inc(s_init, 1)
            nc.vector.memset(UP[:, :, 0:8], 0.0).then_inc(s_init, 1)
            nc.vector.memset(UP[:, :, 8 + S:16 + S], 0.0).then_inc(s_init, 1)
            for t in range(NT):
                norm_tile(0, t)
            nc.vector.tensor_copy(PCOL[:, 0:NCOL], take(("cols",))[:, 0:NCOL]).then_inc(freed["dve"], 1)
            dve.wait_ge(freed["dve"], 1)
            ts(QG1, pcol("q_norm"), HD1 ** -0.5, None, ALU.mult).then_inc(s_cols, 1)
            ts(QG2, pcol("b_q_norm_g_2"), P ** -0.5, None, ALU.mult).then_inc(s_cols, 1)
            split_upto(0)
            norm_split(0, perm=True)
            split_upto(1)
            dve.wait_ge(s_cols, 2)

            def in_final(j):
                q = j < 8
                out_ap = Q1[:, j - 4, ::-1] if q else K1[:, j - 8, :]
                head_final(("in", j), ("inss", j), j - 4, QG1 if q else pcol("k_norm"), out_ap)

            for j in range(12):
                if j % 2 == 0:
                    split_upto(W_IN[j // 2] + 1)
                if j >= 5:
                    in_final(j - 1)
                if j == 10:
                    ada_out(0)
            split_upto(W_V[0][1])
            in_final(11)
            split_upto(W_OUT[0][1])

            dve.wait_ge(s_bias, 16 * 16)
            n_items = len(ITEMS1)
            for j in range(n_items + 3):
                if j < n_items:
                    tr, t, h, kts, n = item1(j)
                    b = take(("a1s", j))
                    if j >= 2:
                        dve.wait_ge(a_exp, j - 1)
                    bias = BIAS[:, h * ROWS:(h + 1) * ROWS, BJ[t]:BJ[t] + n // ROWS].rearrange("p k j -> p j k")
                    tt(S1[j % 2][:, 0:n].rearrange("p (j k) -> p j k", k=ROWS),
                       b[:, 0:n].rearrange("p (j k) -> p j k", k=ROWS), bias, ALU.add).then_inc(freed["dve"], 1)
                    dve.wait_ge(freed["dve"], fills[("a1s", j)][2])
                    nc.vector.tensor_reduce(NM[j % 2], S1[j % 2][:, 0:n], AX.X, ALU.max, negate=True).then_inc(a_nm, 1)
                if 2 <= j < n_items + 2:
                    dve.wait_ge(a_exp, j - 1)
                    if j >= 4:
                        dve.wait_ge(freed["dve"], fills[("a1o", j - 4)][2])
                    nc.vector.reciprocal(RR[j % 2], RS[j % 2]).then_inc(a_rr, 1)
                if j >= 3:
                    tr, t, h, kts, n = item1(j - 3)
                    b = take(("a1o", j - 3))
                    dve.wait_ge(a_rr, j - 2)
                    ts(O1[:, tr, h * HD1:(h + 1) * HD1], b[:, 0:HD1], RR[(j - 3) % 2], None, ALU.mult
                       ).then_inc(freed["dve"], 1)
                if j == 12:
                    ada_out(1)
            ada_gate(2, GATE_A, s_ga)
            for g in range(4):
                split_full(BH[:, g, :], BL[:, g, :], freed["act"], fills[("pool", g)][2])
            dve.wait_ge(filled, fill_no(("ot1", 3)))
            for c in range(4):
                split_full(BH[:, 4 + c, :], BL[:, 4 + c, :], freed["act"], fills[("ot1", c)][2])
            for h in range(2):
                split_upto(W_OUT[h][1] + 1)
                for t in range(NT):
                    part = X[:, t, h * 512:(h + 1) * 512]
                    tt(part, part, take(("wout", h, t))[:, :], ALU.add).then_inc(freed["dve"], 1)
                    if h == 1:
                        norm_behind(1, t)
            for t in range(NT):
                dve.wait_ge(t_hi, t + 1)
                tt(TL[:, t, :], XNORM[1][:, t, :], TH[:, t, :].bitcast(F32), ALU.subtract).then_inc(t_lo, 1)
            nc.vector.memset(POS[:, :, :], 0.0).then_inc(k_step, 1)
            b = take(("logits",))
            dve.wait_ge(r_used, KD)
            lg = b[:, 0:NT * NE].rearrange("p (t e) -> p t e", e=NE)
            nc.vector.tensor_reduce(RMX, lg, AX.X, ALU.max).then_inc(k_step, 1)
            dve.wait_ge(k_step, 2)
            tt(LGX[:, :, :], lg, spread(RMX, NE), ALU.subtract).then_inc(freed["dve"], 1)
            dve.wait_ge(k_exp, 1)
            nc.vector.tensor_reduce(RSM, LGX[:, :, :], AX.X, ALU.add).then_inc(k_step, 1)
            dve.wait_ge(k_step, 3)
            nc.vector.reciprocal(RRC, RSM).then_inc(k_step, 1)
            dve.wait_ge(k_step, 4)
            tt(AFF[:, :, 0:NE], LGX[:, :, :], spread(RRC, NE), ALU.mult).then_inc(k_step, 1)
            nc.vector.tensor_copy(WORK[0][:, :], take(("aff_t",))[0:NE, :]).then_inc(freed["dve"], 1)
            for c in range(2):
                split_full(PH[:, c, :], PL[:, c, :], freed["act"], fills[("pt", c)][2])
            split_upto(W_PROJ)
            dve.wait_ge(freed["dve"], fills[("aff_t",)][2])
            n = 5
            for r in range(CAP // 8):
                nc.vector.max(M8, WORK[r % 2][:, :]).then_inc(k_step, 1)
                n += 1
                dve.wait_ge(k_step, n)
                nc.vector.match_replace(WORK[(r + 1) % 2][:, :], M8, WORK[r % 2][:, :], -1.0).then_inc(k_step, 1)
                n += 1
                dve.wait_ge(k_step, n)
            ts(MASK[:, :], WORK[0][:, :], 0.0, None, ALU.is_lt).then_inc(k_step, 1)
            dve.wait_ge(k_step, n + 1)
            nc.vector.tensor_tensor_scan(WORK[1][:, :], ONEROW, MASK[:, :], 0.0, ALU.mult, ALU.add).then_inc(k_step, 1)
            dve.wait_ge(k_step, n + 2)
            tt(RANK[:, :], WORK[1][:, :], MASK[:, :], ALU.mult).then_inc(k_step, 1)
            nc.vector.tensor_copy(POS[:, :, 0:NE], take(("pos_t",))[:, 0:NT * NE].rearrange("p (t e) -> p t e", e=NE)
                                  ).then_inc(freed["dve"], 1)
            dve.wait_ge(freed["dve"], fills[("pos_t",)][2])

            def select_inputs():
                for t in range(NT):
                    last = ts(SEL[:, t, CAP:2 * CAP], jmod[:, 0:CAP], POSN[:, t:t + 1], None, ALU.is_equal)
                last.then_inc(d_sel, 1)

            dve.wait_ge(freed["act"], COUNT_BEFORE_E["act"])
            nc.vector.memset(SEL[:, :, :].bitcast(F32), 0.0).then_inc(zeroed, 1)
            for x in (SELG[:, :, :], PS[4][:, :], PS[5][:, :]):
                nc.vector.memset(x, 0.0).then_inc(zeroed, 1)
            dve.sem_inc(d_selg, 1)
            nc.vector.tensor_copy(POSN, POS[:, :, 0]).then_inc(d_cur, 1)
            dve.wait_ge(d_cur, 1)
            dve.wait_ge(zeroed, 4)
            select_inputs()

            def add_combined(j, base_):
                t, h = j // 2, j % 2
                dve.wait_ge(m_c, base_ + (j + 1))
                part = X[:, t, h * 512:(h + 1) * 512]
                tt(part, part, PS[6 + j % 2][:, :], ALU.add).then_inc(d_add, 1)

            with dve.Fori(0, NE) as e:
                for i in range(SLABS_E):
                    w = i % 3
                    dve.wait_ge(hi_ready, e * SLABS_E + (WE0 + i + 1))
                    tt(WLO_E[w][:, :], RAW[slot(N_E + i)][:, :], WHI_E[w][:, :].bitcast(F32),
                       ALU.subtract).then_inc(lo_ready, 1)
                    if i == 3:
                        nc.vector.tensor_copy(POSC, POS[:, :, e]).then_inc(d_cur, 1)
                        nc.vector.tensor_copy(AFFC, AFF[:, :, e]).then_inc(d_cur, 1)
                        nc.vector.tensor_copy(POSN, POS[:, :, e + 1]).then_inc(d_cur, 1)
                        dve.wait_ge(d_cur, e * 3 + 4)
                        for t in range(NT):
                            last = ts(SELG[:, t, :], jmod, POSC[:, t:t + 1], AFFC[:, t:t + 1],
                                      ALU.is_equal, ALU.mult)
                        last.then_inc(d_selg, 1)
                        select_inputs()
                    if i in (14, 20):
                        half = 0 if i == 14 else 1
                        dve.wait_ge(v_silu, e * 2 + (half + 1))
                        tt(SQ[1][:, :], SQ[0][:, :], PS[7][:, :], ALU.mult).then_inc(d_prod, 1)
                        dve.wait_ge(d_prod, e * 2 + (half + 1))
                        hid = SQ[1][:, :].rearrange("p (c j) -> p c j", j=CAP)
                        hi = HM[:, 8 * half:8 * half + 8, 0:CAP]
                        nc.vector.tensor_copy(hi, hid).then_inc(d_hi, 1)
                        dve.wait_ge(d_hi, e * 2 + (half + 1))
                        tt(HM[:, 8 * half:8 * half + 8, CAP:P], hid, hi.bitcast(F32), ALU.subtract).then_inc(d_lo, 1)
                    if 4 <= i < 12:
                        add_combined(i - 4, e * 8)
            split_at[0] = WE0 + NE * SLABS_E
            split_upto(W_PGATE[0][1])
            for j in range(8):
                add_combined(j, 8 * NE)
                if j % 2 == 1:
                    norm_behind(2, j // 2)
            dve.wait_ge(e_sq, 4)
            ts(ESS, ESS, 1.0 / D, EPS, ALU.mult, ALU.add).then_inc(k_step, 1)
            dve.wait_ge(k_exp, 2)
            nc.vector.reciprocal(ERSTD, ERSTD).then_inc(k_step, 1)
            norm_split(2)
            dve.wait_ge(k_step, 26)
            dve.wait_ge(s_grow, 32)
            for t in range(NT):
                stt(out=E_[:, t, :], in0=E_[:, t, :], scalar=ERSTD[:, t:t + 1], in1=GROW[:, :],
                    op0=ALU.mult, op1=ALU.mult).then_inc(k_step, 1)
            for h in range(2):
                split_upto(W_PGATE[h][1] + 1)
                for t in range(NT):
                    i = 4 * h + t
                    dve.wait_ge(k_step, 27 + t)
                    dve.wait_ge(freed["act"], fills[("pgate", h, t)][2])
                    r = slice(h * 512, (h + 1) * 512)
                    tt(SQ[i % 2][:, :], SQ[i % 2][:, :], E_[:, t, r], ALU.mult).then_inc(x_mul, 1)
                    dve.wait_ge(x_mul, i + 1)
                    tt(X[:, t, r], X[:, t, r], SQ[i % 2][:, :], ALU.add).then_inc(x_upd, 1)
                    if h == 1:
                        norm_behind(3, t)

            split_upto(W_AV[0][1])
            norm_split(3)
            dve.wait_ge(s_late, 16)
            tril = CL[:, 4 * P:5 * P]
            for i in range(2):
                b = take(("ws", i))
                tt(WST[:, 4 * i:4 * i + 4, :], b[:, :].rearrange("p (g t) -> p g t", g=4), repeat(tril, 4),
                   ALU.mult).then_inc(freed["dve"], 1)
            for h in range(4):
                split_upto(W_AV[h][1] + 1)
                if h == 2:
                    ada_out(3)
            dve.wait_ge(v_sq, 16)
            nc.vector.tensor_reduce(SS, SSV.rearrange("p (t h) -> p t h", h=4), AX.X, ALU.add).then_inc(g_small, 1)
            dve.wait_ge(g_small, 1)
            ts(MS, SS, 1.0 / (2 * D), EPS, ALU.mult, ALU.add).then_inc(g_small, 1)
            dve.wait_ge(v_sq, 17)
            nc.vector.reciprocal(RSTD, STD).then_inc(g_small, 1)
            for g in range(8):
                split_upto(W_AZ[g])
                if g == 0:
                    dve.wait_ge(g_small, 3)
                    for t in range(NT):
                        ts(VV[:, t, :], VV[:, t, :], RSTD[:, t:t + 1], None, ALU.mult).then_inc(g_small, 1)
                split_upto(W_AZ[g] + 1)
                for c in range(2):
                    dve.wait_ge(g_act, 2 * g + c + 1)
                    dve.wait_ge(freed["act"], fills[("az", g, c)][2])
                    tt(SQ[c][:, :], bank(("au", g, c))[:, :], SQ[c][:, :], ALU.mult).then_inc(freed["dve"], 1)
                dve.wait_ge(s_bs[g % 2], 16 * (g // 2 + 1))
                for c in range(2):
                    b = take(("am", g, c))
                    y = FULL[f[0] % 2][:, :]
                    dve.wait_ge(f_lo, f[0] - 1)
                    stt(out=y.rearrange("p (n t) -> p n t", n=NT), in0=b[:, :].rearrange("p (n t) -> p n t", n=NT),
                        scalar=pcol("a_sgu_g_2", 2 * g + c), in1=repeat(BS[g % 2][:, :], NT), op0=ALU.mult, op1=ALU.add
                        ).then_inc(freed["dve"], 1)
                    dve.wait_ge(freed["dve"], fills[("am", g, c)][2])
                    tt(y, y, SQ[c][:, :], ALU.mult).then_inc(g_mul, 1)
                    kc = (2 * g + c) % KD
                    split_full(BH[:, kc, :], BL[:, kc, :], g_mul, 2 * g + c + 1)
                if g in (0, 2, 4):
                    ada_out(4 + g // 2)
                if g == 7:
                    ada_gate(7, GATE_B, s_gb)
                if g % 4 == 3:
                    for h in range(2):
                        split_upto(W_AO[g // 4][h][1] + 1)
                        dve.wait_ge(g_mul, 2 * g + 2)
                        gated_out([("ao", g // 4, h, t) for t in range(NT)], GATE_A, 4 if g == 7 and h == 1 else None)

            norm_split(4)
            for j in range(6):
                if j % 2 == 0:
                    split_upto(W_K[j // 2] + 1)
                if j >= 1:
                    k2_final(dve, head_final, j - 1)
            split_upto(W_VK[0] + 1)
            k2_final(dve, head_final, 5)
            for g in range(1, NG):
                split_upto(W_VK[g] + 1)
            norm_split(5)
            for g in range(NG):
                for j in range(H2):
                    if j % 2 == 0:
                        split_upto(W_Q[g][j // 2] + 1)
                    if j >= 1:
                        q2_final(dve, head_final, g, j - 1)
                q2_final(dve, head_final, g, 7)
                split_upto(W_Q[g][3] + 2)
                dve.wait_ge(freed["dve"], fills[("q2", g, 7)][2])
                dist = (CL[:, 0:2 * P], CL[:, 2 * P:3 * P], CL[:, 3 * P:4 * P])[g]
                n_items, j0, tag = NT * H2, 32 * (g + 1), f"b{g}"
                for j in range(n_items + 3):
                    if j < n_items:
                        t, h, kts, n = item2(g, j)
                        b = take((tag + "s", j))
                        if j >= 2:
                            dve.wait_ge(a_exp, j0 + j - 1)
                        d = dist[:, P:2 * P] if g == 0 and n == P else dist[:, 0:n]
                        stt(out=S2[j % 2][:, 0:n], in0=d, scalar=-slopes[g * H2 + h], in1=b[:, 0:n],
                            op0=ALU.mult, op1=ALU.add).then_inc(freed["dve"], 1)
                        dve.wait_ge(freed["dve"], fills[(tag + "s", j)][2])
                        nc.vector.tensor_reduce(NM2[:, g, j:j + 1], S2[j % 2][:, 0:n], AX.X, ALU.max, negate=True
                                                ).then_inc(a_nm, 1)
                    if j >= 3:
                        t, h, _, _ = item2(g, j - 3)
                        nc.vector.tensor_copy(O2[g][:, h, t, :], take((tag + "o", j - 3))[:, 0:P]).then_inc(freed["dve"], 1)
            for g in range(NG):
                for key, dst in ((("nm_t", g), NT2), (("l_t", g), LT2)):
                    nc.vector.tensor_copy(to_order(dst[g][:, :], g), in_order(take(key)[0:H2, :], g)).then_inc(freed["dve"], 1)
            dve.wait_ge(freed["dve"], fills[("l_t", NG - 1)][2])
            tt(MIN2[:, :], NT2[0][:, :], NT2[1][:, :], ALU.min).then_inc(c_step, 1)
            dve.wait_ge(c_step, 1)
            tt(MIN2[:, :], MIN2[:, :], NT2[2][:, :], ALU.min).then_inc(c_step, 1)
            dve.wait_ge(c_step, 2)
            for g in range(NG):
                tt(NT2[g][:, :], MIN2[:, :], NT2[g][:, :], ALU.subtract).then_inc(c_step, 1)
            for g in range(NG):
                dve.wait_ge(c_exp, g + 1)
                tt(LT2[g][:, :], LT2[g][:, :], NT2[g][:, :], ALU.mult).then_inc(c_step, 1)
            dve.wait_ge(c_step, 8)
            tt(MIN2[:, :], LT2[0][:, :], LT2[1][:, :], ALU.add).then_inc(c_step, 1)
            dve.wait_ge(c_step, 9)
            tt(MIN2[:, :], MIN2[:, :], LT2[2][:, :], ALU.add).then_inc(c_step, 1)
            dve.wait_ge(c_step, 10)
            nc.vector.reciprocal(MIN2[:, :], MIN2[:, :]).then_inc(c_step, 1)
            dve.wait_ge(c_step, 11)
            for g in range(NG):
                tt(in_order(LT2[g][:, :], g), to_order(NT2[g][:, :], g), to_order(MIN2[:, :], g), ALU.mult).then_inc(c_step, 1)
            for g in range(NG):
                nc.vector.tensor_copy(NM2[:, g, :], take(("wg", g))[:, 0:NT * H2]).then_inc(freed["dve"], 1)
            dve.wait_ge(freed["dve"], fills[("wg", NG - 1)][2])

            def diagonals(h):
                for g in range(NG):
                    for t in range(NT):
                        ts(DG[h % 2][:, g * NT + t, :], ident, NM2[:, g, t * H2 + h:t * H2 + h + 1], None,
                           ALU.mult).then_inc(c_step, 1)

            diagonals(0)
            for h in range(H2):
                if h % 2 == 0:
                    split_upto(W_Z[h // 2] + 1)
                if h + 1 < H2:
                    if h >= 1:
                        dve.wait_ge(filled, fill_no(("comb", h - 1)))
                    diagonals(h + 1)
                b = take(("comb", h))
                dve.wait_ge(freed["act"], fills[("z", h)][2])
                dve.wait_ge(f_lo, f[0] - 1)
                tt(FULL[f[0] % 2][:, :], SQ[h % 2][:, :], b[:, :], ALU.mult).then_inc(freed["dve"], 1)
                split_full(BH[:, h, :], BL[:, h, :], freed["dve"], fills[("comb", h)][2])
            for h in range(2):
                split_upto(min(W_BO[h][1] + 1, len(n_of["W"]) - 1))
                gated_out([("bo", h, t) for t in range(NT)], GATE_B)


_OUTS = [((1, S, D), "float32")]


def kernel(**inputs):
    import numpy as _np
    import concourse.bacc as _bacc
    from concourse import mybir as _mybir
    from concourse.bass_utils import run_bass_kernel_spmd as _run

    nc = _bacc.Bacc("TRN2", target_bir_lowering=False, num_devices=1)
    arrays, args = {}, {}
    for name in inputs:
        x = _np.ascontiguousarray(inputs[name])
        arrays[f"in_{name}"] = x
        args[name] = nc.dram_tensor(f"in_{name}", x.shape, _mybir.dt.from_np(x.dtype), kind="ExternalInput").ap()
    shape, dtype = _OUTS[0]
    out = nc.dram_tensor("out_0", shape, _mybir.dt.from_np(_np.dtype(dtype)), kind="ExternalOutput").ap()
    bass_kernel(nc, args, out)
    r = _run(nc, [arrays], core_ids=[0])
    return r.results[0]["out_0"]
```
